# Optimizing a Trainium2 kernel written in Bass

```python
import jax, jax.numpy as jnp
from jax import lax
import numpy as np

D_MODEL = 1024
BATCH = 1
SEQ = 2048
DEPTH = 1

HEAD_DIM = 64
N_Q_HEADS = 8
N_KV_HEADS = 2
GROUP = N_Q_HEADS // N_KV_HEADS
ATTN_WIDTH = N_Q_HEADS * HEAD_DIM
KV_WIDTH = N_KV_HEADS * HEAD_DIM
WINDOW = 128
BLOCK = 128
ROT_DIM = HEAD_DIM // 4
ROPE_THETA = 500000.0
CONV_WIDTH = D_MODEL - ATTN_WIDTH
CONV_K = 3
MIX_WIDTH = ATTN_WIDTH + CONV_WIDTH
IN_SPLITS = [ATTN_WIDTH, KV_WIDTH, KV_WIDTH, ATTN_WIDTH,
             CONV_WIDTH, CONV_WIDTH, CONV_WIDTH, CONV_WIDTH]
IN_WIDTH = sum(IN_SPLITS)
EPS = 1e-5

kernel_name = "hybrid_swa_sink_shortconv_block"

def rms_norm(x, g):
    xf = x.astype(jnp.float32)
    y = xf * lax.rsqrt(jnp.mean(xf * xf, axis=-1, keepdims=True) + EPS)
    return (y * g.astype(jnp.float32)).astype(x.dtype)

def partial_rope(t, pos):
    half = ROT_DIM // 2
    inv_freq = ROPE_THETA ** (-jnp.arange(0, ROT_DIM, 2, dtype=jnp.float32) / ROT_DIM)
    ang = pos.astype(jnp.float32)[:, None] * inv_freq[None, :]
    cos = jnp.cos(ang)[None, :, None, :]
    sin = jnp.sin(ang)[None, :, None, :]
    rot = t[..., :ROT_DIM].astype(jnp.float32)
    x1, x2 = rot[..., :half], rot[..., half:]
    r = jnp.concatenate([x1 * cos - x2 * sin, x2 * cos + x1 * sin], axis=-1)
    return jnp.concatenate([r.astype(t.dtype), t[..., ROT_DIM:]], axis=-1)

def sliding_window_sink_attention(q, k, v, sinks):
    B, S, _, D = q.shape
    nb = S // BLOCK
    qb = q.reshape(B, nb, BLOCK, N_KV_HEADS, GROUP, D)
    kb = k.reshape(B, nb, BLOCK, N_KV_HEADS, D)
    vb = v.reshape(B, nb, BLOCK, N_KV_HEADS, D)
    pad = ((0, 0), (1, 0), (0, 0), (0, 0), (0, 0))
    kk = jnp.concatenate([jnp.pad(kb, pad)[:, :-1], kb], axis=2)
    vv = jnp.concatenate([jnp.pad(vb, pad)[:, :-1], vb], axis=2)
    scale = 1.0 / np.sqrt(D)
    s = jnp.einsum('bnqkgd,bnskd->bnkgqs', qb, kk,
                   preferred_element_type=jnp.float32) * scale
    qi = jnp.arange(BLOCK)[:, None]
    kj = jnp.arange(2 * BLOCK)[None, :]
    delta = qi + BLOCK - kj
    band = (delta >= 0) & (delta < WINDOW)
    valid = (jnp.arange(nb)[:, None] * BLOCK + kj - BLOCK) >= 0
    mask = (band[None] & valid[:, None, :])[None, :, None, None]
    s = jnp.where(mask, s, -jnp.inf)
    sink = sinks.astype(jnp.float32).reshape(N_KV_HEADS, GROUP)[None, None, :, :, None, None]
    m = jnp.maximum(jnp.max(s, axis=-1, keepdims=True), sink)
    p = jnp.exp(s - m)
    denom = jnp.sum(p, axis=-1, keepdims=True) + jnp.exp(sink - m)
    prob = (p / denom).astype(v.dtype)
    o = jnp.einsum('bnkgqs,bnskd->bnqkgd', prob, vv,
                   preferred_element_type=jnp.float32)
    return o.reshape(B, S, N_Q_HEADS * D).astype(q.dtype)

def causal_short_conv(u, w):
    S = u.shape[1]
    up = jnp.pad(u, ((0, 0), (CONV_K - 1, 0), (0, 0)))
    y = w[0] * up[:, 0:S]
    for j in range(1, CONV_K):
        y = y + w[j] * up[:, j:j + S]
    return y

def setup_inputs(seed: int = 0) -> dict:
    key = jax.random.key(seed)
    ks = jax.random.split(key, 8)
    f32 = jnp.float32
    x = jax.random.normal(ks[0], (BATCH, SEQ, D_MODEL), f32)
    norm_g = 1.0 + 0.02 * jax.random.normal(ks[1], (D_MODEL,), f32)
    w_in = jax.random.normal(ks[2], (D_MODEL, IN_WIDTH), f32) * D_MODEL ** -0.5
    sinks = 0.5 * jax.random.normal(ks[3], (N_Q_HEADS,), f32)
    conv_w = jax.random.normal(ks[4], (CONV_K, CONV_WIDTH), f32) * CONV_K ** -0.5
    w_out = jax.random.normal(ks[5], (MIX_WIDTH, D_MODEL), f32) * MIX_WIDTH ** -0.5
    final_g = 1.0 + 0.02 * jax.random.normal(ks[6], (D_MODEL,), f32)
    return {"x": x, "norm_g": norm_g, "w_in": w_in, "sinks": sinks,
            "conv_w": conv_w, "w_out": w_out, "final_g": final_g}

def reference(x, norm_g, w_in, sinks, conv_w, w_out, final_g):
    B, S, _ = x.shape
    pos = jnp.arange(S, dtype=jnp.int32)
    h = x
    for _ in range(DEPTH):
        xn = rms_norm(h, norm_g)
        proj = jnp.einsum('bsd,de->bse', xn, w_in)
        offs = list(np.cumsum(IN_SPLITS)[:-1])
        q, k, v, g_attn, b_gate, c_gate, h_in, g_conv = jnp.split(proj, offs, axis=-1)
        q = partial_rope(q.reshape(B, S, N_Q_HEADS, HEAD_DIM), pos)
        k = partial_rope(k.reshape(B, S, N_KV_HEADS, HEAD_DIM), pos)
        v = v.reshape(B, S, N_KV_HEADS, HEAD_DIM)
        attn = sliding_window_sink_attention(q, k, v, sinks)
        y_attn = attn * jax.nn.silu(g_attn)
        y_conv = b_gate * causal_short_conv(c_gate * h_in, conv_w)
        y_conv = y_conv * jax.nn.silu(g_conv)
        mix = jnp.concatenate([y_attn, y_conv], axis=-1)
        h = h + jnp.einsum('bse,ed->bsd', mix, w_out)
    return rms_norm(h, final_g)


_drawn_inputs = setup_inputs


def setup_inputs(seed=0):
    import zlib

    import numpy as np

    out = dict(_drawn_inputs(seed))
    spreads = {}
    factors = {'norm_g': 3.397, 'sinks': 64.0, 'final_g': 7.503}
    for name, (base, spread) in spreads.items():
        noise = np.random.default_rng([zlib.crc32(name.encode()), seed]).standard_normal(out[name].shape)
        drawn = base * np.exp(spread * noise) if base else spread * noise
        out[name] = __import__('jax').numpy.asarray(drawn.astype(out[name].dtype))
    for name, factor in factors.items():
        out[name] = (out[name] * factor).astype(out[name].dtype)
    return out
```

```python
from contextlib import ExitStack

import concourse.bass as bass
from concourse import mybir

ALU = mybir.AluOpType
ACT = mybir.ActivationFunctionType
F32 = mybir.dt.float32
F32R = mybir.dt.float32r

P = 128
D_MODEL = 1024
SEQ = 2048
HEAD_DIM = 64
N_Q_HEADS = 8
N_KV_HEADS = 2
GROUP = N_Q_HEADS // N_KV_HEADS
CONV_K = 3
ROT_DIM = HEAD_DIM // 4
EPS = 1e-5
SCALE = HEAD_DIM ** -0.5
MASKED = -3.0e38

T = 512
CHUNKS = SEQ // T
BLOCKS = T // P
KT = D_MODEL // P
PAIRS = N_Q_HEADS // 2
CONVS = 4
UNITS = N_KV_HEADS * BLOCKS

COL = {"Q": 0, "K": 4, "V": 5, "A": 6, "B": 10, "C": 14, "H": 18, "G": 22}
ITEMS = [("K", 0), ("V", 0), ("Q", 0), ("Q", 1),
         ("H", 0), ("C", 0), ("G", 0), ("B", 0),
         ("Q", 2), ("Q", 3),
         ("H", 1), ("C", 1), ("G", 1), ("B", 1),
         ("H", 2), ("C", 2), ("G", 2), ("B", 2),
         ("A", 0), ("A", 1),
         ("H", 3), ("C", 3), ("G", 3), ("B", 3),
         ("A", 2), ("A", 3)] + [("O", m) for m in range(KT)]
N = len(ITEMS)
N_IN = N - KT
RING3 = [j % 3 for j in range(N - 1)] + [1]
MADE = [i for i in ITEMS if i[0] in "BA"]
MIX_TILE = {i: (i[1] if i[0] == "A" else PAIRS + i[1]) for i in MADE}
GATES = [i for i in ITEMS if i[0] in "GA"]
ROPED = [i for i in ITEMS if i[0] in "KQ"]
KQV = [i for i in ITEMS if i[0] in "KQV"]
FROM_ACT = [i for i in ITEMS if i[0] in "KVQHO"]

V_TURN = 3
QK_SLOT = [6 + 2 * u for u in range(UNITS)]
TURN_SLOT = [s + 2 for s in QK_SLOT]
PV_SLOT = [s + 3 for s in QK_SLOT]
SQUARE_SLOT = [9, 11, 13, 15]
SCALE_SLOT = [17, 18, 19, 20]

STEPS_ROPE = 4
STEPS_CONV = 6


def at(c, per, k):
    return c * per + k


def primed(c, per, k):
    return c * per + per + k


def wait_alone(eng, sem, value, passed):
    eng.wait_ge(sem, value)
    eng.sem_inc(passed, 1)


def before(j):
    for back in (0, 1):
        for i in range(j - 1 if not back else N - 1, -1, -1):
            if RING3[i] == RING3[j]:
                return i, back


def hybrid_layer(nc, x, norm_g, w_in, sinks, conv_w, w_out, final_g, rope, out):
    with ExitStack() as ctx:
        def sb(name, shape, dt=F32):
            return ctx.enter_context(nc.sbuf_tensor(name, shape, dt))

        def ps(name, shape):
            return ctx.enter_context(nc.psum_tensor(name, shape, F32))

        def sem(name):
            return ctx.enter_context(nc.semaphore(name))

        w_raw = sb("w_raw", [P, 3, KT, P])
        w_split = sb("w_split", [P, 2, 2, KT, P], F32R)
        xn_hi = sb("xn_hi", [P, KT, T], F32R)
        xn_lo = sb("xn_lo", [P, KT, T], F32R)
        mix_hi = sb("mix_hi", [P, KT, T], F32R)
        mix_lo = sb("mix_lo", [P, KT, T], F32R)
        x_next = sb("x_next", [P, BLOCKS, D_MODEL])
        h = sb("h", [P, BLOCKS, D_MODEL])
        q_st = sb("q_st", [P, N_Q_HEADS, T], F32R)
        k_st = sb("k_st", [P, 4, P + T], F32R)
        v_st = sb("v_st", [P, 1 + BLOCKS, N_KV_HEADS, 2, HEAD_DIM], F32R)
        rope_t = sb("rope_t", [P, 2, T])
        kq_raw = sb("kq_raw", [P, 2, T])
        rot_a = sb("rot_a", [P, T])
        rot_b = sb("rot_b", [P, T])
        probs = sb("probs", [P, GROUP, 2 * P])
        pt_hi = sb("pt_hi", [P, 2, GROUP * P], F32R)
        pt_lo = sb("pt_lo", [P, 2, GROUP * P], F32R)
        attn = sb("attn", [P, PAIRS, T])
        h_in = sb("h_in", [P, T])
        u = sb("u", [P, CONV_K - 1 + T])
        u_tail = sb("u_tail", [P, CONVS, CONV_K - 1])
        y = sb("y", [P, T])
        th = sb("th", [P, T])
        y_out = sb("y_out", [P, 2, T])
        ident = sb("ident", [P, P])
        band = sb("band", [P, 2 * P])
        band_0 = sb("band_0", [P, 2 * P])
        vec_rows = sb("vec_rows", [KT + CONV_K * CONVS, P])
        vecs = sb("vecs", [P, KT + CONV_K * CONVS])
        g_fin = sb("g_fin", [P, D_MODEL])
        sink = sb("sink", [P, N_Q_HEADS])
        neg_sink = sb("neg_sink", [P, N_Q_HEADS])
        neg_max = sb("neg_max", [P, GROUP])
        sink_off = sb("sink_off", [P, GROUP])
        sink_exp = sb("sink_exp", [P, GROUP])
        row_sum = sb("row_sum", [P, GROUP])
        denom = sb("denom", [P, GROUP])
        inv = sb("inv", [P, GROUP])
        sq_in = sb("sq_in", [P, BLOCKS])
        mean_in = sb("mean_in", [P, BLOCKS])
        r_in = sb("r_in", [P, BLOCKS])
        sq_fin = sb("sq_fin", [P, BLOCKS])
        mean_fin = sb("mean_fin", [P, BLOCKS])
        r_fin = sb("r_fin", [P, BLOCKS])
        minus_half = sb("minus_half", [P, BLOCKS])

        g_in = vecs[:, 0:KT]
        taps = vecs[:, KT:].rearrange("p (w t) -> p w t", w=CONV_K)

        ps_proj = [ps(f"ps_proj{i}", [P, T]) for i in range(3)]
        ps_s = ps("ps_s", [P, 2, T])
        ps_t = ps("ps_t", [P, 2, T])
        ps_o = ps("ps_o", [P, T])

        w_in_sbuf = [sem(f"w_in_sbuf{i}") for i in range(3)]
        rows_in = sem("rows_in")
        consts_in = sem("consts_in")
        rope_in = sem("rope_in")
        x_first = [sem(f"x_first{t}") for t in range(BLOCKS)]
        x_in = sem("x_in")
        h_in_sbuf = sem("h_in_sbuf")
        stored = sem("stored")
        proj_done = sem("proj_done")
        rows_turned = sem("rows_turned")
        v_turned = sem("v_turned")
        qk_done = sem("qk_done")
        p_turned = sem("p_turned")
        pv_done = sem("pv_done")
        x_turned = sem("x_turned")
        y_turned = sem("y_turned")
        vecs_done = sem("vecs_done")
        w_hi = sem("w_hi")
        copied = sem("copied")
        kq_hi = sem("kq_hi")
        v_hi = sem("v_hi")
        kept = sem("kept")
        exp_done = sem("exp_done")
        pt_hi_done = sem("pt_hi_done")
        o_copied = sem("o_copied")
        tanh_done = sem("tanh_done")
        mix_hi_done = sem("mix_hi_done")
        xn_hi_done = sem("xn_hi_done")
        squared = sem("squared")
        w_lo = sem("w_lo")
        rope_step = sem("rope_step")
        kq_lo = sem("kq_lo")
        v_lo = sem("v_lo")
        max_done = sem("max_done")
        off_done = sem("off_done")
        norm_step = sem("norm_step")
        p_ready = sem("p_ready")
        pt_lo_done = sem("pt_lo_done")
        o_added = sem("o_added")
        conv_step = sem("conv_step")
        silu_done = sem("silu_done")
        gated = sem("gated")
        made = sem("made")
        mix_lo_done = sem("mix_lo_done")
        x_scaled = sem("x_scaled")
        xn_lo_done = sem("xn_lo_done")
        h_added = sem("h_added")
        finished = sem("finished")
        signs = sem("signs")
        consts_made = sem("consts_made")
        mean_in_done = sem("mean_in_done")
        r_in_done = sem("r_in_done")
        mean_fin_done = sem("mean_fin_done")
        r_fin_done = sem("r_fin_done")
        band_done = sem("band_done")

        pool_passed = sem("pool_passed")
        dve_passed = sem("dve_passed")

        x_dram = x.rearrange("b (t p) d -> p (b t) d", p=P)
        out_dram = out.rearrange("b (t p) d -> p (b t) d", p=P)
        w_in_dram = w_in.rearrange("(k p) e -> p k e", p=P)
        w_out_dram = w_out.rearrange("(k p) e -> p k e", p=P)

        def item_dram(j):
            kind, n = ITEMS[j]
            if kind == "O":
                return w_out_dram[:, :, n * P:(n + 1) * P]
            col = (COL[kind] + n) * P
            return w_in_dram[:, :, col:col + P]

        def came(j):
            return RING3[:j + 1].count(RING3[j]), RING3.count(RING3[j])

        def released(j):
            kind, n = ITEMS[j]
            if kind in "KVQHO":
                return copied, len(FROM_ACT), FROM_ACT.index(ITEMS[j]) + 1
            if kind == "C":
                return conv_step, STEPS_CONV * CONVS, STEPS_CONV * n + 2
            if kind in "GA":
                return silu_done, len(GATES), GATES.index(ITEMS[j]) + 1
            return made, len(MADE), MADE.index(ITEMS[j]) + 1

        def squares(c, last, of_result, k):
            if last or not of_result:
                return c * 2 * BLOCKS + BLOCKS + k
            return c * 2 * BLOCKS + 2 * BLOCKS + k

        def by_chunk(eng, body):
            with eng.Fori(0, CHUNKS - 1) as c:
                body(c, False)
            body(CHUNKS - 1, True)

        block = ctx.enter_context(nc.Block())

        @block.sync
        def _(sp):
            for t in range(BLOCKS):
                sp.dma_start(x_next[:, t], x_dram[:, t]).then_inc(x_first[t], 16)
            sp.dma_start(vec_rows[0:KT, :], norm_g.rearrange("(k p) -> k p", p=P)).then_inc(rows_in, 16)
            sp.dma_start(vec_rows[KT:, :], conv_w.rearrange("w (t p) -> (w t) p", p=P)).then_inc(rows_in, 16)

            def body(c, last):
                for j in range(N):
                    i, back = before(j)
                    count, per = came(j)
                    sp.wait_ge(w_lo, primed(c, N, i + 1 - N * back))
                    sp.dma_start(w_raw[:, RING3[j]], item_dram(j)).then_inc(w_in_sbuf[RING3[j]], 16)
                    if j == 0:
                        sp.wait_ge(rope_step, primed(c, STEPS_ROPE * len(ROPED), 0))
                        sp.dma_start(rope_t[:, :, :], rope[:, bass.ds(c, 1)].rearrange("p o a t -> p (o a) t")).then_inc(rope_in, 16)

            by_chunk(sp, body)

        @block.gpsimd
        def _(pool):
            pool.dma_start(sink[:, :], sinks.partition_broadcast(P)).then_inc(consts_in, 16)
            pool.dma_start(g_fin[:, :], final_g.partition_broadcast(P)).then_inc(consts_in, 16)
            pool.memset(ident[:, :], 0.0).then_inc(consts_made, 1)
            pool.memset(minus_half[:, :], -0.5).then_inc(consts_made, 1)
            pool.memset(u_tail[:, :, :], 0.0).then_inc(consts_made, 1)
            pool.memset(band[:, :], 0.0).then_inc(consts_made, 1)
            pool.wait_ge(consts_made, 4)
            pool.affine_select(out=ident[:, :], in_=ident[:, :], compare_op=ALU.not_equal, fill=1.0,
                               base=0, pattern=[[-1, P]], channel_multiplier=1).then_inc(consts_made, 1)
            pool.affine_select(out=band[:, :], in_=band[:, :], compare_op=ALU.is_ge, fill=MASKED,
                               base=-1, pattern=[[1, 2 * P]], channel_multiplier=-1).then_inc(consts_made, 1)
            pool.wait_ge(consts_made, 6)
            pool.affine_select(out=band[:, :], in_=band[:, :], compare_op=ALU.is_ge, fill=MASKED,
                               base=P, pattern=[[-1, 2 * P]], channel_multiplier=1).then_inc(consts_made, 1)
            pool.memset(band_0[:, 0:P], MASKED).then_inc(consts_made, 1)
            pool.wait_ge(consts_made, 8)
            pool.tensor_copy(band_0[:, P:], band[:, P:]).then_inc(consts_made, 1)
            pool.dma_start(h[:, :, :], x_dram[:, 0:BLOCKS]).then_inc(h_in_sbuf, 16)
            pool.sem_inc(band_done, 1)

            def inverse_norm(c, sums, mean, r, sums_done, mean_done, r_done):
                wait_alone(pool, squared, sums_done, pool_passed)
                pool.tensor_scalar(mean[:, :], sums[:, :], 1.0 / D_MODEL, EPS, ALU.mult,
                                   ALU.add).then_inc(mean_done, 1)
                wait_alone(pool, mean_done, at(c, 1, 1), pool_passed)
                pool.tensor_tensor(r[:, :], mean[:, :], minus_half[:, :], ALU.pow).then_inc(r_done, 1)

            inverse_norm(0, sq_in, mean_in, r_in, BLOCKS, mean_in_done, r_in_done)

            def body(c, last):
                if not last:
                    wait_alone(pool, x_turned, at(c, KT, KT), pool_passed)
                    pool.dma_start(x_next[:, :, :], x_dram[:, bass.ds((c + 1) * BLOCKS, BLOCKS)])\
                        .then_inc(x_in, 16)
                if not last:
                    inverse_norm(c + 1, sq_in, mean_in, r_in, squares(c, last, False, BLOCKS), mean_in_done,
                                 r_in_done)
                    wait_alone(pool, max_done, at(c, UNITS * GROUP, (BLOCKS + 1) * GROUP), pool_passed)
                    pool.tensor_copy(band_0[:, 0:P], band[:, 0:P]).then_inc(band_done, 1)
                inverse_norm(c, sq_fin, mean_fin, r_fin, squares(c, last, True, BLOCKS), mean_fin_done,
                             r_fin_done)
                wait_alone(pool, finished, at(c, BLOCKS, BLOCKS), pool_passed)
                pool.dma_start(out_dram[:, bass.ds(c * BLOCKS, BLOCKS)], h[:, :, :]).then_inc(stored, 16)
                if not last:
                    wait_alone(pool, stored, at(c, 16, 16), pool_passed)
                    pool.dma_start(h[:, :, :], x_dram[:, bass.ds((c + 1) * BLOCKS, BLOCKS)])\
                        .then_inc(h_in_sbuf, 16)

            by_chunk(pool, body)
            pool.wait_ge(stored, 16 * CHUNKS)

        @block.scalar
        def _(act):
            def split_w(c, j):
                count, per = came(j)
                act.wait_ge(w_in_sbuf[RING3[j]], at(c, 16 * per, 16 * count))
                act.wait_ge(proj_done, primed(c, N, j - 1))
                act.activation(w_split[:, j % 2, 0], w_raw[:, RING3[j]], ACT.Copy).then_inc(w_hi, 1)

            def square(src, t, dst, before):
                if not (isinstance(before, int) and before == 0):
                    act.wait_ge(squared, before)
                act.activation(junk, src[:, t], ACT.Square, accum_out=dst[:, t:t + 1]).then_inc(squared, 1)

            junk = y_out[:, :, :].rearrange("p a t -> p (a t)")

            def turn_x(c, k):
                act.wait_ge(x_turned, at(c, KT, k + 1))
                act.activation(xn_hi[:, k], ps_t[:, k % 2], ACT.Copy, scale=g_in[:, k:k + 1])\
                    .then_inc(xn_hi_done, 1)

            def copy_out(c, last, j):
                kind, n = ITEMS[j]
                if kind not in "KVQHOGA":
                    return
                act.wait_ge(proj_done, primed(c, N, j + 1))
                src = ps_proj[RING3[j]]
                if kind in "KVQ":
                    turn = KQV.index((kind, n)) % 2
                    if (kind, n) == ("Q", 1):
                        act.wait_ge(v_turned, at(c, 1, 1))
                    act.activation(kq_raw[:, turn], src[:, :], ACT.Copy).then_inc(copied, 1)
                elif kind == "H":
                    act.activation(h_in[:, :], src[:, :], ACT.Copy).then_inc(copied, 1)
                elif kind == "O":
                    if n == 0:
                        act.wait_ge(squared, squares(c, last, True, 0))
                    if n >= 2:
                        act.wait_ge(y_turned, at(c, KT, n - 1))
                    act.activation(y_out[:, n % 2], src[:, :], ACT.Copy).then_inc(copied, 1)
                else:
                    act.activation(th[:, :], src[:, :], ACT.Tanh, scale=0.5).then_inc(tanh_done, 1)

            def high_part(c, j):
                kind, n = ITEMS[j]
                if kind in "KQ":
                    i = ROPED.index((kind, n))
                    act.wait_ge(rope_step, primed(c, STEPS_ROPE * len(ROPED), STEPS_ROPE * (i + 1)))
                if kind == "K":
                    act.activation(k_st[:, :, 0:P], k_st[:, :, T:T + P].bitcast(F32), ACT.Copy)\
                        .then_inc(kept, 1)
                    act.wait_ge(kept, at(c, 2, 1))
                    for kv in range(N_KV_HEADS):
                        src = rot_a[kv * HEAD_DIM:(kv + 1) * HEAD_DIM, :]
                        for half in range(2):
                            ins = act.activation(k_st[half * HEAD_DIM:(half + 1) * HEAD_DIM, 2 * kv, P:],
                                                 src, ACT.Copy)
                    ins.then_inc(kq_hi, 1)
                elif kind == "Q":
                    act.activation(q_st[0:HEAD_DIM, 2 * n], rot_a[0:HEAD_DIM, :], ACT.Copy)
                    act.activation(q_st[HEAD_DIM:P, 2 * n + 1], rot_a[HEAD_DIM:P, :], ACT.Copy)\
                        .then_inc(kq_hi, 1)
                elif kind in "BA":
                    act.wait_ge(made, primed(c, len(MADE), MADE.index((kind, n)) + 1))
                    act.activation(mix_hi[:, MIX_TILE[kind, n]], y[:, :], ACT.Copy, scale=0.5)\
                        .then_inc(mix_hi_done, 1)

            def v_high(c):
                act.wait_ge(v_turned, at(c, 1, 1))
                act.activation(v_st[:, 0], v_st[:, BLOCKS].bitcast(F32), ACT.Copy).then_inc(kept, 1)
                act.wait_ge(kept, at(c, 2, 2))
                act.activation(v_st[:, 1:, :, 0, :],
                               ps_o[:, :].rearrange("p (b k d) -> p b k d", b=BLOCKS, k=N_KV_HEADS),
                               ACT.Copy).then_inc(v_hi, 1)

            def exps(c, un):
                for i in range(GROUP):
                    act.wait_ge(max_done, at(c, UNITS * GROUP, un * GROUP + i + 1))
                    act.activation(probs[:, i], probs[:, i], ACT.Exp, bias=neg_max[:, i:i + 1],
                                   scale=-1.0, accum_out=row_sum[:, i:i + 1])
                act.wait_ge(off_done, at(c, UNITS, un + 1))
                act.activation(sink_exp[:, :], sink_off[:, :], ACT.Exp).then_inc(exp_done, 1)

            def probs_high(c, un):
                for kb in range(2):
                    act.wait_ge(p_turned, at(c, 2 * UNITS, 2 * un + kb + 1))
                    act.activation(pt_hi[:, kb], ps_t[:, kb], ACT.Copy).then_inc(pt_hi_done, 1)

            def copy_o(c, un):
                g, b = divmod(un, BLOCKS)
                pair = slice(g * GROUP // 2, (g + 1) * GROUP // 2)
                o = ps_o[:, :].rearrange("p (i e q) -> p i e q", i=GROUP // 2, e=2)
                act.wait_ge(pv_done, at(c, UNITS, un + 1))
                act.activation(attn[HEAD_DIM:P, pair, b * P:(b + 1) * P], o[0:HEAD_DIM, :, 1], ACT.Copy)
                act.activation(attn[0:HEAD_DIM, pair, b * P:(b + 1) * P], o[HEAD_DIM:P, :, 0], ACT.Copy)\
                    .then_inc(o_copied, 1)

            act.sem_inc(copied, len(FROM_ACT))
            for t in range(BLOCKS):
                act.wait_ge(x_first[t], 16)
                square(x_next, t, sq_in, t)
            split_w(0, 0)
            act.wait_ge(rows_turned, 1)
            act.activation(vecs[:, :], ps_o[:, 0:KT + CONV_K * CONVS], ACT.Copy).then_inc(vecs_done, 1)
            act.wait_ge(vecs_done, 1)
            for k in range(KT):
                turn_x(0, k)
            split_w(0, 1)

            def body(c, last):
                for s in range(N):
                    if s > 0 and s + 1 < N:
                        split_w(c, s + 1)
                    elif s + 1 == N and not last:
                        split_w(c + 1, 0)
                    if s >= 2 and s != N_IN + 1:
                        high_part(c, s - 2)
                    if s >= 1:
                        copy_out(c, last, s - 1)
                    if s == N_IN:
                        high_part(c, s - 1)
                    if s == V_TURN:
                        v_high(c)
                    if s in TURN_SLOT:
                        probs_high(c, TURN_SLOT.index(s))
                    if s in QK_SLOT:
                        exps(c, QK_SLOT.index(s))
                    if s in PV_SLOT:
                        copy_o(c, PV_SLOT.index(s))
                    if not last and s in SQUARE_SLOT:
                        t = SQUARE_SLOT.index(s)
                        if t == 0:
                            act.wait_ge(x_in, at(c + 1, 16, 0))
                        square(x_next, t, sq_in, squares(c, last, False, t))
                    if not last and N_IN <= s < N_IN + KT // 2:
                        turn_x(c + 1, 2 * (s - N_IN))
                        turn_x(c + 1, 2 * (s - N_IN) + 1)
                copy_out(c, last, N - 1)
                if not last:
                    split_w(c + 1, 1)
                act.wait_ge(y_turned, at(c, KT, KT))
                act.wait_ge(h_added, primed(c, KT, KT))
                for t in range(BLOCKS):
                    square(h, t, sq_fin, squares(c, last, True, t))

            by_chunk(act, body)

        @block.vector
        def _(dve):
            def split_w(c, j):
                dve.wait_ge(w_hi, at(c, N, j + 1))
                dve.tensor_tensor(w_split[:, j % 2, 1], w_raw[:, RING3[j]],
                                  w_split[:, j % 2, 0].bitcast(F32), ALU.subtract).then_inc(w_lo, 1)

            def scale_x(c, t):
                if t == 0:
                    dve.wait_ge(r_in_done, at(c, 1, 1))
                dve.tensor_scalar(x_next[:, t], x_next[:, t], r_in[:, t:t + 1], None, ALU.mult)\
                    .then_inc(x_scaled, 1)

            def turn_x(c, k):
                dve.wait_ge(xn_hi_done, at(c, KT, k + 1))
                dve.scalar_tensor_tensor(xn_lo[:, k], ps_t[:, k % 2], g_in[:, k:k + 1],
                                         xn_hi[:, k].bitcast(F32), ALU.mult, ALU.subtract)\
                    .then_inc(xn_lo_done, 1)

            def rotate(c, j):
                kind, n = ITEMS[j]
                i = ROPED.index((kind, n))
                turn = KQV.index((kind, n)) % 2
                done = STEPS_ROPE * i
                per = STEPS_ROPE * len(ROPED)
                src = kq_raw[:, turn]
                if i == 0:
                    dve.wait_ge(rope_in, at(c, 16, 16))
                dve.wait_ge(copied, primed(c, len(FROM_ACT), FROM_ACT.index((kind, n)) + 1))
                dve.wait_ge(kq_lo, primed(c, len(ROPED), i))
                half = ROT_DIM // 2
                swap = [p ^ half if p < ROT_DIM else p for p in range(32)]
                dve.tensor_tensor(rot_a[:, :], src, rope_t[:, 0], ALU.mult).then_inc(rope_step, 1)
                dve.stream_shuffle(rot_b[:, :], src, swap).then_inc(rope_step, 1)
                dve.wait_ge(rope_step, primed(c, per, done + 2))
                dve.tensor_tensor(rot_b[:, :], rot_b[:, :], rope_t[:, 1], ALU.mult).then_inc(rope_step, 1)
                dve.wait_ge(rope_step, primed(c, per, done + 3))
                dve.tensor_tensor(rot_a[:, :], rot_a[:, :], rot_b[:, :], ALU.add).then_inc(rope_step, 1)

            def y_free(c, item):
                dve.wait_ge(mix_lo_done, primed(c, len(MADE), MADE.index(item)))

            def convolve(c, n):
                per, done = STEPS_CONV * CONVS, STEPS_CONV * n
                bank = ps_proj[RING3[ITEMS.index(("C", n))]]
                lag = CONV_K - 1
                dve.wait_ge(proj_done, primed(c, N, ITEMS.index(("C", n)) + 1))
                dve.wait_ge(copied, primed(c, len(FROM_ACT), FROM_ACT.index(("H", n)) + 1))
                dve.wait_ge(conv_step, primed(c, per, done))
                dve.tensor_copy(u[:, 0:lag], u_tail[:, n]).then_inc(conv_step, 1)
                dve.tensor_tensor(u[:, lag:], bank[:, :], h_in[:, :], ALU.mult).then_inc(conv_step, 1)
                dve.wait_ge(conv_step, primed(c, per, done + 2))
                y_free(c, ("B", n))
                dve.tensor_scalar(y[:, :], u[:, 0:T], taps[:, 0, n:n + 1], None, ALU.mult)\
                    .then_inc(conv_step, 1)
                for j in range(1, CONV_K):
                    dve.wait_ge(conv_step, primed(c, per, done + 2 + j))
                    dve.scalar_tensor_tensor(y[:, :], u[:, j:j + T], taps[:, j, n:n + 1], y[:, :],
                                             ALU.mult, ALU.add).then_inc(conv_step, 1)
                dve.tensor_copy(u_tail[:, n], u[:, T:T + lag]).then_inc(conv_step, 1)

            def gate(c, j):
                kind, n = ITEMS[j]
                i = GATES.index((kind, n))
                dve.wait_ge(tanh_done, at(c, len(GATES), i + 1))
                dve.scalar_tensor_tensor(th[:, :], th[:, :], 1.0, ps_proj[RING3[j]][:, :],
                                         ALU.add, ALU.mult).then_inc(silu_done, 1)
                if kind == "A":
                    dve.wait_ge(o_added, primed(c, UNITS, BLOCKS * (n // (GROUP // 2) + 1)))
                    dve.wait_ge(silu_done, primed(c, len(GATES), i + 1))
                    y_free(c, (kind, n))
                    dve.tensor_tensor(y[:, :], th[:, :], attn[:, n], ALU.mult).then_inc(made, 1)
                else:
                    dve.wait_ge(conv_step, primed(c, STEPS_CONV * CONVS, STEPS_CONV * n + 5))
                    dve.wait_ge(silu_done, primed(c, len(GATES), i + 1))
                    dve.tensor_tensor(y[:, :], th[:, :], y[:, :], ALU.mult).then_inc(gated, 1)

            def times_b(c, j):
                n = ITEMS[j][1]
                dve.wait_ge(proj_done, primed(c, N, j + 1))
                dve.wait_ge(gated, at(c, CONVS, n + 1))
                dve.tensor_tensor(y[:, :], ps_proj[RING3[j]][:, :], y[:, :], ALU.mult).then_inc(made, 1)

            def add_h(c, m):
                if m == 0:
                    dve.wait_ge(h_in_sbuf, at(c, 16, 16))
                dve.wait_ge(y_turned, at(c, KT, m + 1))
                dst = h[:, :, m * P:(m + 1) * P]
                dve.tensor_tensor(dst, ps_s[:, m % 2].rearrange("p (t d) -> p t d", t=BLOCKS), dst,
                                  ALU.add).then_inc(h_added, 1)

            def low_part(c, j):
                kind, n = ITEMS[j]
                lo, hi = slice(0, HEAD_DIM), slice(HEAD_DIM, P)
                if kind in "KQ":
                    dve.wait_ge(kq_hi, at(c, len(ROPED), ROPED.index((kind, n)) + 1))
                if kind == "K":
                    for kv, own in enumerate((lo, hi)):
                        for half in (lo, hi):
                            ins = dve.tensor_tensor(k_st[half, 2 * kv + 1, P:], rot_a[own, :],
                                                    k_st[own, 2 * kv, P:].bitcast(F32), ALU.subtract)
                    ins.then_inc(kq_lo, 1)
                elif kind == "Q":
                    dve.tensor_tensor(q_st[hi, 2 * n], rot_a[lo, :], q_st[lo, 2 * n].bitcast(F32),
                                      ALU.subtract)
                    dve.tensor_tensor(q_st[lo, 2 * n + 1], rot_a[hi, :], q_st[hi, 2 * n + 1].bitcast(F32),
                                      ALU.subtract).then_inc(kq_lo, 1)
                elif kind in "BA":
                    k = MIX_TILE[kind, n]
                    dve.wait_ge(mix_hi_done, at(c, len(MADE), MADE.index((kind, n)) + 1))
                    dve.scalar_tensor_tensor(mix_lo[:, k], y[:, :], 0.5, mix_hi[:, k].bitcast(F32),
                                             ALU.mult, ALU.subtract).then_inc(mix_lo_done, 1)

            def v_low(c):
                dve.wait_ge(v_hi, at(c, 1, 1))
                dve.tensor_tensor(v_st[:, 1:, :, 1, :],
                                  ps_o[:, :].rearrange("p (b k d) -> p b k d", b=BLOCKS, k=N_KV_HEADS),
                                  v_st[:, 1:, :, 0, :].bitcast(F32), ALU.subtract).then_inc(v_lo, 1)

            def maxima(c, un):
                g, b = divmod(un, BLOCKS)
                mask = band_0 if b == 0 else band
                if un == 0:
                    wait_alone(dve, band_done, primed(c, 1, 0), dve_passed)
                wait_alone(dve, qk_done, at(c, UNITS, un + 1), dve_passed)
                for i in range(GROUP):
                    head = g * GROUP + i
                    dve.tensor_tensor_reduce(
                        out=probs[:, i], in0=ps_s[:, i // 2, (i % 2) * 2 * P:(i % 2 + 1) * 2 * P],
                        in1=mask[:, :], scale=-SCALE, scalar=neg_sink[:, head:head + 1],
                        op0=ALU.add, op1=ALU.min, accum_out=neg_max[:, i:i + 1]).then_inc(max_done, 1)
                dve.wait_ge(max_done, at(c, UNITS * GROUP, (un + 1) * GROUP))
                dve.tensor_tensor(sink_off[:, :], neg_max[:, :], sink[:, g * GROUP:(g + 1) * GROUP],
                                  ALU.add).then_inc(off_done, 1)

            def normalize(c, un):
                dve.wait_ge(exp_done, at(c, UNITS, un + 1))
                dve.tensor_tensor(denom[:, :], row_sum[:, :], sink_exp[:, :], ALU.add)\
                    .then_inc(norm_step, 1)
                dve.wait_ge(norm_step, at(c, 2 * UNITS, 2 * un + 1))
                dve.reciprocal(inv[:, :], denom[:, :]).then_inc(norm_step, 1)
                dve.wait_ge(norm_step, at(c, 2 * UNITS, 2 * un + 2))
                for i in range(GROUP):
                    ins = dve.tensor_scalar(probs[:, i], probs[:, i], inv[:, i:i + 1], None, ALU.mult)
                ins.then_inc(p_ready, 1)

            def probs_low(c, un):
                for kb in range(2):
                    dve.wait_ge(pt_hi_done, at(c, 2 * UNITS, 2 * un + kb + 1))
                    dve.tensor_tensor(pt_lo[:, kb], ps_t[:, kb], pt_hi[:, kb].bitcast(F32),
                                      ALU.subtract).then_inc(pt_lo_done, 1)

            def add_o(c, un):
                g, b = divmod(un, BLOCKS)
                pair = slice(g * GROUP // 2, (g + 1) * GROUP // 2)
                o = ps_o[:, :].rearrange("p (i e q) -> p i e q", i=GROUP // 2, e=2)
                dve.wait_ge(o_copied, at(c, UNITS, un + 1))
                for e, half in enumerate((slice(0, HEAD_DIM), slice(HEAD_DIM, P))):
                    dst = attn[half, pair, b * P:(b + 1) * P]
                    ins = dve.tensor_tensor(dst, o[half, :, e], dst, ALU.add)
                ins.then_inc(o_added, 1)

            for primed_sem, per in ((w_lo, N), (rope_step, STEPS_ROPE * len(ROPED)),
                                    (conv_step, STEPS_CONV * CONVS), (silu_done, len(GATES)),
                                    (made, len(MADE)), (o_added, UNITS), (h_added, KT),
                                    (kq_lo, len(ROPED)), (mix_lo_done, len(MADE))):
                dve.sem_inc(primed_sem, per)
            dve.memset(k_st[:, :, T:T + P].bitcast(F32), 0.0)
            dve.memset(v_st[:, BLOCKS].bitcast(F32), 0.0).then_inc(signs, 1)
            dve.wait_ge(consts_in, 32)
            dve.tensor_scalar(neg_sink[:, :], sink[:, :], -1.0, None, ALU.mult).then_inc(signs, 1)
            for t in range(BLOCKS):
                scale_x(0, t)
            split_w(0, 0)
            dve.wait_ge(vecs_done, 1)
            for k in range(KT):
                turn_x(0, k)
            split_w(0, 1)
            dve.wait_ge(signs, 2)
            dve.wait_ge(consts_made, 9)

            def body(c, last):
                for s in range(N):
                    if s > 0 and s + 1 < N:
                        split_w(c, s + 1)
                    elif s + 1 == N and not last:
                        split_w(c + 1, 0)
                    if s >= 2 and s != N_IN + 1:
                        low_part(c, s - 2)
                    if s >= 1:
                        kind, n = ITEMS[s - 1]
                        if kind in "KQ":
                            rotate(c, s - 1)
                        elif kind == "C":
                            convolve(c, n)
                        elif kind in "GA":
                            gate(c, s - 1)
                        elif kind == "B":
                            times_b(c, s - 1)
                    if s == N_IN:
                        low_part(c, s - 1)
                    if s == V_TURN:
                        v_low(c)
                    if s in TURN_SLOT:
                        probs_low(c, TURN_SLOT.index(s))
                    if s in QK_SLOT:
                        maxima(c, QK_SLOT.index(s))
                    if s - 1 in QK_SLOT:
                        normalize(c, QK_SLOT.index(s - 1))
                    if s in PV_SLOT:
                        add_o(c, PV_SLOT.index(s))
                    if not last and s in SCALE_SLOT:
                        scale_x(c + 1, SCALE_SLOT.index(s))
                    if not last and N_IN <= s < N_IN + KT // 2:
                        turn_x(c + 1, 2 * (s - N_IN))
                        turn_x(c + 1, 2 * (s - N_IN) + 1)
                    if s > N_IN + 1:
                        add_h(c, s - N_IN - 2)
                add_h(c, KT - 2)
                add_h(c, KT - 1)
                if not last:
                    split_w(c + 1, 1)
                dve.wait_ge(r_fin_done, at(c, 1, 1))
                for t in range(BLOCKS):
                    dve.scalar_tensor_tensor(h[:, t], h[:, t], r_fin[:, t:t + 1], g_fin[:, :],
                                             ALU.mult, ALU.mult).then_inc(finished, 1)

            by_chunk(dve, body)

        @block.tensor
        def _(pe):
            def product(c, j):
                kind, n = ITEMS[j]
                i, back = before(j)
                pe.wait_ge(w_lo, primed(c, N, j + 1))
                bank_free, per, k = released(i)
                pe.wait_ge(bank_free, primed(c, per, k - per * back))
                hi, lo = (mix_hi, mix_lo) if kind == "O" else (xn_hi, xn_lo)
                order = [MIX_TILE[i] for i in MADE] if kind == "O" else range(KT)
                for a, k in enumerate(order):
                    if j == 0 and a == 0:
                        pe.wait_ge(xn_lo_done, at(c, KT, KT))
                    if kind == "O" and n == 0:
                        pe.wait_ge(mix_lo_done, primed(c, len(MADE), a + 1))
                    for b, (w, v) in enumerate(((0, hi), (0, lo), (1, hi))):
                        mm = pe.matmul(ps_proj[RING3[j]][:, :], w_split[:, j % 2, w, k], v[:, k],
                                       start=a == 0 and b == 0, stop=a == KT - 1 and b == 2)
                mm.then_inc(proj_done, 1)

            def turn_v(c):
                pe.wait_ge(copied, primed(c, len(FROM_ACT), FROM_ACT.index(("V", 0)) + 1))
                pe.wait_ge(o_added, primed(c, UNITS, 0))
                for b in range(BLOCKS):
                    mm = pe.transpose(ps_o[:, b * P:(b + 1) * P], kq_raw[:, 1, b * P:(b + 1) * P], ident[:, :])
                mm.then_inc(v_turned, 1)

            def scores(c, un):
                g, b = divmod(un, BLOCKS)
                pe.wait_ge(kq_lo, primed(c, len(ROPED), 1 + (g + 1) * GROUP // 2))
                if un == 0:
                    pe.wait_ge(h_added, primed(c, KT, 0))
                for i in range(GROUP):
                    for part in range(2):
                        mm = pe.matmul(ps_s[:, i // 2, (i % 2) * 2 * P:(i % 2 + 1) * 2 * P],
                                       q_st[:, g * GROUP + i, b * P:(b + 1) * P],
                                       k_st[:, 2 * g + part, b * P:(b + 2) * P],
                                       start=part == 0, stop=part == 1)
                mm.then_inc(qk_done, 1)

            def turn_p(c, un):
                pe.wait_ge(p_ready, at(c, UNITS, un + 1))
                for kb in range(2):
                    for i in range(GROUP):
                        mm = pe.transpose(ps_t[:, kb, i * P:(i + 1) * P], probs[:, i, kb * P:(kb + 1) * P],
                                          ident[:, :])
                    mm.then_inc(p_turned, 1)

            def values(c, un):
                g, b = divmod(un, BLOCKS)
                if un == 0:
                    pe.wait_ge(v_lo, at(c, 1, 1))
                else:
                    pe.wait_ge(o_added, primed(c, UNITS, un))
                for kb in range(2):
                    pe.wait_ge(pt_lo_done, at(c, 2 * UNITS, 2 * un + kb + 1))
                    for part, pt in enumerate((pt_hi, pt_lo)):
                        mm = pe.matmul(ps_o[:, :],
                                       v_st[:, b + kb, g].rearrange("p a d -> p (a d)"), pt[:, kb],
                                       start=kb == 0 and part == 0, stop=kb == 1 and part == 1)
                mm.then_inc(pv_done, 1)

            def turn_x(c, k):
                if k == 0:
                    pe.wait_ge(x_scaled, at(c, BLOCKS, BLOCKS))
                if k >= 2:
                    pe.wait_ge(xn_lo_done, at(c, KT, k - 1))
                for t in range(BLOCKS):
                    mm = pe.transpose(ps_t[:, k % 2, t * P:(t + 1) * P], x_next[:, t, k * P:(k + 1) * P],
                                      ident[:, :])
                mm.then_inc(x_turned, 1)

            def turn_y(c, m):
                pe.wait_ge(copied, primed(c, len(FROM_ACT), FROM_ACT.index(("O", m)) + 1))
                if m >= 2:
                    pe.wait_ge(h_added, primed(c, KT, m - 1))
                for t in range(BLOCKS):
                    mm = pe.transpose(ps_s[:, m % 2, t * P:(t + 1) * P], y_out[:, m % 2, t * P:(t + 1) * P],
                                      ident[:, :])
                mm.then_inc(y_turned, 1)

            pe.sem_inc(proj_done, N)
            pe.wait_ge(consts_made, 7)
            pe.wait_ge(rows_in, 32)
            pe.transpose(ps_o[:, 0:KT + CONV_K * CONVS], vec_rows[:, :],
                         ident[0:KT + CONV_K * CONVS, 0:KT + CONV_K * CONVS]).then_inc(rows_turned, 1)
            for k in range(KT):
                turn_x(0, k)

            def body(c, last):
                for s in range(N):
                    if s == V_TURN:
                        turn_v(c)
                    if s in PV_SLOT:
                        values(c, PV_SLOT.index(s))
                    if s in TURN_SLOT:
                        turn_p(c, TURN_SLOT.index(s))
                    if s in QK_SLOT:
                        scores(c, QK_SLOT.index(s))
                    if not last and N_IN <= s < N_IN + KT // 2:
                        turn_x(c + 1, 2 * (s - N_IN))
                        turn_x(c + 1, 2 * (s - N_IN) + 1)
                    product(c, s)
                    if s > N_IN:
                        turn_y(c, s - N_IN - 1)
                turn_y(c, KT - 1)

            by_chunk(pe, body)


_INS = ["x", "norm_g", "w_in", "sinks", "conv_w", "w_out", "final_g"]


def rope_tables():
    import numpy as np
    half = ROT_DIM // 2
    inv_freq = np.float32(500000.0) ** (-np.arange(0, ROT_DIM, 2, dtype=np.float32) / np.float32(ROT_DIM))
    ang = np.arange(SEQ, dtype=np.float32)[None, :] * inv_freq.astype(np.float32)[:, None]
    cos, sin = np.cos(ang.astype(np.float64)), np.sin(ang.astype(np.float64))
    table = np.zeros((2, HEAD_DIM, SEQ), np.float64)
    table[0] = 1.0
    table[0, :ROT_DIM] = np.concatenate([cos, cos])
    table[1, :ROT_DIM] = np.concatenate([-sin, sin])
    table = np.concatenate([table] * (P // HEAD_DIM), axis=1).reshape(2, P, CHUNKS, T)
    return np.ascontiguousarray(table.transpose(1, 2, 0, 3).astype(np.float32))


def kernel(**inputs):
    import numpy as np
    import concourse.bacc as bacc
    from concourse.bass_utils import run_bass_kernel_spmd

    nc = bacc.Bacc("TRN2", target_bir_lowering=False, num_devices=1)
    arrays, args = {}, []
    for name, a in [(n, inputs[n]) for n in _INS] + [("rope", rope_tables())]:
        a = np.ascontiguousarray(a)
        arrays[f"in_{name}"] = a
        args.append(nc.dram_tensor(f"in_{name}", a.shape, mybir.dt.from_np(a.dtype), kind="ExternalInput").ap())
    args.append(nc.dram_tensor("out_0", (1, SEQ, D_MODEL), F32, kind="ExternalOutput").ap())
    hybrid_layer(nc, *args)
    r = run_bass_kernel_spmd(nc, [arrays], core_ids=[0])
    return r.results[0]["out_0"]
```

```python
from contextlib import ExitStack

import concourse.bass as bass
from concourse import mybir

ALU = mybir.AluOpType
ACT = mybir.ActivationFunctionType
F32 = mybir.dt.float32
F32R = mybir.dt.float32r

P = 128
D_MODEL = 1024
SEQ = 2048
HEAD_DIM = 64
N_Q_HEADS = 8
N_KV_HEADS = 2
GROUP = N_Q_HEADS // N_KV_HEADS
CONV_K = 3
ROT_DIM = HEAD_DIM // 4
EPS = 1e-5
SCALE = HEAD_DIM ** -0.5
MASKED = -3.0e38

T = 512
CHUNKS = SEQ // T
BLOCKS = T // P
KT = D_MODEL // P
PAIRS = N_Q_HEADS // 2
CONVS = 4
UNITS = N_KV_HEADS * BLOCKS

COL = {"Q": 0, "K": 4, "V": 5, "A": 6, "B": 10, "C": 14, "H": 18, "G": 22}
ITEMS = [("K", 0), ("V", 0), ("Q", 0), ("Q", 1),
         ("H", 0), ("C", 0), ("G", 0), ("B", 0),
         ("Q", 2), ("Q", 3),
         ("H", 1), ("C", 1), ("G", 1), ("B", 1),
         ("H", 2), ("C", 2), ("G", 2), ("B", 2),
         ("A", 0), ("A", 1),
         ("H", 3), ("C", 3), ("G", 3), ("B", 3),
         ("A", 2), ("A", 3)] + [("O", m) for m in range(KT)]
N = len(ITEMS)
N_IN = N - KT
RING3 = [j % 3 for j in range(N - 1)] + [1]
MADE = [i for i in ITEMS if i[0] in "BA"]
MIX_TILE = {i: (i[1] if i[0] == "A" else PAIRS + i[1]) for i in MADE}
GATES = [i for i in ITEMS if i[0] in "GA"]
ROPED = [i for i in ITEMS if i[0] in "KQ"]
KQV = [i for i in ITEMS if i[0] in "KQV"]
FROM_ACT = [i for i in ITEMS if i[0] in "KVQHO"]

V_TURN = 3
HEAD = 8
QK_SLOT = [7 + 2 * u for u in range(UNITS)]
TURN_SLOT = [s + 2 for s in QK_SLOT]
PV_SLOT = [s + 3 for s in QK_SLOT]
RESULT_SLOT = [2, 2, 4, 4]
FINISH_SLOT = [4, 5, 6, 7]
SQUARE_SLOT = [14, 16, 18, 20]
SCALE_SLOT = [22, 23, 24, 25]

STEPS_ROPE = 4
STEPS_CONV = 6


def at(c, per, k):
    return c * per + k


def primed(c, per, k):
    return c * per + per + k


def wait_alone(eng, sem, value, passed):
    eng.wait_ge(sem, value)
    eng.sem_inc(passed, 1)


def before(j):
    for back in (0, 1):
        for i in range(j - 1 if not back else N - 1, -1, -1):
            if RING3[i] == RING3[j]:
                return i, back


def hybrid_layer(nc, x, norm_g, w_in, sinks, conv_w, w_out, final_g, rope, out):
    with ExitStack() as ctx:
        def sb(name, shape, dt=F32):
            return ctx.enter_context(nc.sbuf_tensor(name, shape, dt))

        def ps(name, shape):
            return ctx.enter_context(nc.psum_tensor(name, shape, F32))

        def sem(name):
            return ctx.enter_context(nc.semaphore(name))

        w_raw = sb("w_raw", [P, 3, KT, P])
        w_split = sb("w_split", [P, 2, 2, KT, P], F32R)
        xn_hi = sb("xn_hi", [P, KT, T], F32R)
        xn_lo = sb("xn_lo", [P, KT, T], F32R)
        mix_hi = sb("mix_hi", [P, KT, T], F32R)
        mix_lo = sb("mix_lo", [P, KT, T], F32R)
        x_next = sb("x_next", [P, BLOCKS, D_MODEL])
        h = sb("h", [P, BLOCKS, D_MODEL])
        q_st = sb("q_st", [P, N_Q_HEADS, T], F32R)
        k_st = sb("k_st", [P, 4, P + T], F32R)
        v_st = sb("v_st", [P, 1 + BLOCKS, N_KV_HEADS, 2, HEAD_DIM], F32R)
        rope_t = sb("rope_t", [P, 2, T])
        kq_raw = sb("kq_raw", [P, 2, T])
        rot_a = sb("rot_a", [P, T])
        rot_b = sb("rot_b", [P, T])
        probs = sb("probs", [P, GROUP, 2 * P])
        pt_hi = sb("pt_hi", [P, 2, GROUP * P], F32R)
        pt_lo = sb("pt_lo", [P, 2, GROUP * P], F32R)
        attn = sb("attn", [P, PAIRS, T])
        h_in = sb("h_in", [P, T])
        u = sb("u", [P, CONV_K - 1 + T])
        u_tail = sb("u_tail", [P, CONVS, CONV_K - 1])
        y = sb("y", [P, T])
        th = sb("th", [P, T])
        y_out = sb("y_out", [P, 2, T])
        ident = sb("ident", [P, P])
        band = sb("band", [P, 2 * P])
        band_0 = sb("band_0", [P, 2 * P])
        vec_rows = sb("vec_rows", [KT + CONV_K * CONVS, P])
        vecs = sb("vecs", [P, KT + CONV_K * CONVS])
        g_fin = sb("g_fin", [P, D_MODEL])
        sink = sb("sink", [P, N_Q_HEADS])
        neg_sink = sb("neg_sink", [P, N_Q_HEADS])
        neg_max = sb("neg_max", [P, GROUP])
        sink_off = sb("sink_off", [P, GROUP])
        sink_exp = sb("sink_exp", [P, GROUP])
        row_sum = sb("row_sum", [P, GROUP])
        denom = sb("denom", [P, GROUP])
        inv = sb("inv", [P, GROUP])
        sq_in = sb("sq_in", [P, BLOCKS])
        mean_in = sb("mean_in", [P, BLOCKS])
        r_in = sb("r_in", [P, BLOCKS])
        sq_fin = sb("sq_fin", [P, BLOCKS])
        mean_fin = sb("mean_fin", [P, BLOCKS])
        r_fin = sb("r_fin", [P, BLOCKS])
        sq_rest = sb("sq_rest", [P, BLOCKS])
        minus_half = sb("minus_half", [P, BLOCKS])

        g_in = vecs[:, 0:KT]
        taps = vecs[:, KT:].rearrange("p (w t) -> p w t", w=CONV_K)

        ps_proj = [ps(f"ps_proj{i}", [P, T]) for i in range(3)]
        ps_s = ps("ps_s", [P, 2, T])
        ps_t = ps("ps_t", [P, 2, T])
        ps_o = ps("ps_o", [P, T])

        w_in_sbuf = [sem(f"w_in_sbuf{i}") for i in range(3)]
        rows_in = sem("rows_in")
        consts_in = sem("consts_in")
        rope_in = sem("rope_in")
        x_first = [sem(f"x_first{t}") for t in range(BLOCKS)]
        x_in = sem("x_in")
        h_in_sbuf = sem("h_in_sbuf")
        stored = sem("stored")
        stored_last = sem("stored_last")
        proj_done = sem("proj_done")
        rows_turned = sem("rows_turned")
        v_turned = sem("v_turned")
        qk_done = sem("qk_done")
        p_turned = sem("p_turned")
        pv_done = sem("pv_done")
        x_turned = sem("x_turned")
        y_turned = sem("y_turned")
        vecs_done = sem("vecs_done")
        w_hi = sem("w_hi")
        copied = sem("copied")
        kq_hi = sem("kq_hi")
        v_hi = sem("v_hi")
        kept = sem("kept")
        exp_done = sem("exp_done")
        pt_hi_done = sem("pt_hi_done")
        o_copied = sem("o_copied")
        tanh_done = sem("tanh_done")
        mix_hi_done = sem("mix_hi_done")
        xn_hi_done = sem("xn_hi_done")
        squared = sem("squared")
        w_lo = sem("w_lo")
        rope_step = sem("rope_step")
        kq_lo = sem("kq_lo")
        v_lo = sem("v_lo")
        max_done = sem("max_done")
        off_done = sem("off_done")
        norm_step = sem("norm_step")
        p_ready = sem("p_ready")
        pt_lo_done = sem("pt_lo_done")
        o_added = sem("o_added")
        conv_step = sem("conv_step")
        silu_done = sem("silu_done")
        gated = sem("gated")
        made = sem("made")
        mix_lo_done = sem("mix_lo_done")
        x_scaled = sem("x_scaled")
        xn_lo_done = sem("xn_lo_done")
        h_added = sem("h_added")
        finished = sem("finished")
        last_mean_done = sem("last_mean_done")
        gained = sem("gained")
        last_scaled = [sem("last_scaled_dve"), sem("last_scaled_act")]
        signs = sem("signs")
        consts_made = sem("consts_made")
        mean_in_done = sem("mean_in_done")
        r_in_done = sem("r_in_done")
        mean_fin_done = sem("mean_fin_done")
        r_fin_done = sem("r_fin_done")
        band_done = sem("band_done")

        pool_passed = sem("pool_passed")
        dve_passed = sem("dve_passed")

        x_dram = x.rearrange("b (t p) d -> p (b t) d", p=P)
        out_dram = out.rearrange("b (t p) d -> p (b t) d", p=P)
        w_in_dram = w_in.rearrange("(k p) e -> p k e", p=P)
        w_out_dram = w_out.rearrange("(k p) e -> p k e", p=P)

        def item_dram(j):
            kind, n = ITEMS[j]
            if kind == "O":
                return w_out_dram[:, :, n * P:(n + 1) * P]
            col = (COL[kind] + n) * P
            return w_in_dram[:, :, col:col + P]

        def came(j):
            return RING3[:j + 1].count(RING3[j]), RING3.count(RING3[j])

        def released(j):
            kind, n = ITEMS[j]
            if kind in "KVQHO":
                return copied, len(FROM_ACT), FROM_ACT.index(ITEMS[j]) + 1
            if kind == "C":
                return conv_step, STEPS_CONV * CONVS, STEPS_CONV * n + 2
            if kind in "GA":
                return silu_done, len(GATES), GATES.index(ITEMS[j]) + 1
            return made, len(MADE), MADE.index(ITEMS[j]) + 1

        def squares(c, of_result, k):
            return c * 2 * BLOCKS + BLOCKS + (BLOCKS if of_result else 0) + k

        def turn_bank(c, k):
            if isinstance(c, int) and c == 0:
                return (ps_t, ps_s)[k // 2 % 2][:, k % 2]
            return ps_t[:, k % 2]

        LAST_SQUARES = squares(CHUNKS - 1, False, 0)
        LAST_PART = 6

        def by_chunk(eng, slots):
            slots(0, range(HEAD), True)
            with eng.Fori(0, CHUNKS - 1) as c:
                slots(c, range(HEAD, N), False)
                slots(c + 1, range(HEAD), False)
            slots(CHUNKS - 1, range(HEAD, N), True)

        block = ctx.enter_context(nc.Block())

        @block.sync
        def _(sp):
            for t in range(BLOCKS):
                sp.dma_start(x_next[:, t], x_dram[:, t]).then_inc(x_first[t], 16)
            sp.dma_start(vec_rows[0:KT, :], norm_g.rearrange("(k p) -> k p", p=P)).then_inc(rows_in, 16)
            sp.dma_start(vec_rows[KT:, :], conv_w.rearrange("w (t p) -> (w t) p", p=P)).then_inc(rows_in, 16)

            def slots(c, these, edge):
                for j in these:
                    i, back = before(j)
                    count, per = came(j)
                    sp.wait_ge(w_lo, primed(c, N, i + 1 - N * back))
                    sp.dma_start(w_raw[:, RING3[j]], item_dram(j)).then_inc(w_in_sbuf[RING3[j]], 16)
                    if j == 1:
                        sp.wait_ge(rope_step, primed(c, STEPS_ROPE * len(ROPED), 0))
                        sp.dma_start(rope_t[:, :, :], rope[:, bass.ds(c, 1)].rearrange("p o a t -> p (o a) t"))\
                            .then_inc(rope_in, 16)

            by_chunk(sp, slots)
            for t in range(BLOCKS):
                sp.wait_ge(last_scaled[t % 2], t // 2 + 1)
                sp.dma_start(out_dram[:, (CHUNKS - 1) * BLOCKS + t], x_next[:, t]).then_inc(stored_last, 16)
            sp.wait_ge(stored_last, 16 * BLOCKS)

        @block.gpsimd
        def _(pool):
            pool.dma_start(sink[:, :], sinks.partition_broadcast(P)).then_inc(consts_in, 16)
            pool.memset(ident[:, :], 0.0).then_inc(consts_made, 1)
            pool.memset(minus_half[:, :], -0.5).then_inc(consts_made, 1)
            pool.memset(u_tail[:, :, :], 0.0).then_inc(consts_made, 1)
            pool.memset(band[:, :], 0.0).then_inc(consts_made, 1)
            pool.wait_ge(consts_made, 4)
            pool.affine_select(out=ident[:, :], in_=ident[:, :], compare_op=ALU.not_equal, fill=1.0,
                               base=0, pattern=[[-1, P]], channel_multiplier=1).then_inc(consts_made, 1)
            pool.affine_select(out=band[:, :], in_=band[:, :], compare_op=ALU.is_ge, fill=MASKED,
                               base=-1, pattern=[[1, 2 * P]], channel_multiplier=-1).then_inc(consts_made, 1)
            pool.wait_ge(consts_made, 6)
            pool.affine_select(out=band[:, :], in_=band[:, :], compare_op=ALU.is_ge, fill=MASKED,
                               base=P, pattern=[[-1, 2 * P]], channel_multiplier=1).then_inc(consts_made, 1)
            pool.memset(band_0[:, 0:P], MASKED).then_inc(consts_made, 1)
            pool.wait_ge(consts_made, 8)
            pool.tensor_copy(band_0[:, P:], band[:, P:]).then_inc(consts_made, 1)
            pool.sem_inc(band_done, 1)

            for t in range(BLOCKS):
                col = slice(t, t + 1)
                pool.wait_ge(squared, t + 1)
                pool.tensor_scalar(mean_in[:, col], sq_in[:, col], 1.0 / D_MODEL, EPS, ALU.mult,
                                   ALU.add).then_inc(mean_in_done, 1)
                pool.wait_ge(mean_in_done, t + 1)
                pool.tensor_tensor(r_in[:, col], mean_in[:, col], minus_half[:, col], ALU.pow)\
                    .then_inc(r_in_done, 1)

            pool.dma_start(g_fin[:, :], final_g.partition_broadcast(P)).then_inc(consts_in, 16)
            pool.dma_start(h[:, :, :], x_dram[:, 0:BLOCKS]).then_inc(h_in_sbuf, 16)

            def inverse_norm(c, sums, mean, r, sums_done, mean_done, r_done):
                wait_alone(pool, squared, sums_done, pool_passed)
                pool.tensor_scalar(mean[:, :], sums[:, :], 1.0 / D_MODEL, EPS, ALU.mult,
                                   ALU.add).then_inc(mean_done, 1)
                wait_alone(pool, mean_done, c, pool_passed)
                pool.tensor_tensor(r[:, :], mean[:, :], minus_half[:, :], ALU.pow).then_inc(r_done, 1)

            with pool.Fori(0, CHUNKS - 1) as c:
                wait_alone(pool, x_turned, at(c, KT, KT), pool_passed)
                pool.dma_start(x_next[:, :, :], x_dram[:, bass.ds((c + 1) * BLOCKS, BLOCKS)])\
                    .then_inc(x_in, 16)
                inverse_norm(c + 1 + BLOCKS, sq_in, mean_in, r_in, squares(c, False, BLOCKS),
                             mean_in_done, r_in_done)
                wait_alone(pool, max_done, at(c, UNITS * GROUP, (BLOCKS + 1) * GROUP), pool_passed)
                pool.tensor_copy(band_0[:, 0:P], band[:, 0:P]).then_inc(band_done, 1)
                inverse_norm(c + 1, sq_fin, mean_fin, r_fin, squares(c, True, BLOCKS),
                             mean_fin_done, r_fin_done)
                wait_alone(pool, finished, at(c, BLOCKS, BLOCKS), pool_passed)
                pool.dma_start(out_dram[:, bass.ds(c * BLOCKS, BLOCKS)], h[:, :, :]).then_inc(stored, 16)
                wait_alone(pool, stored, at(c, 16, 16), pool_passed)
                pool.dma_start(h[:, :, :], x_dram[:, bass.ds((c + 1) * BLOCKS, BLOCKS)])\
                    .then_inc(h_in_sbuf, 16)
            pool.wait_ge(last_mean_done, 2)
            pool.tensor_tensor(r_fin[:, :], mean_fin[:, :], minus_half[:, :], ALU.pow).then_inc(r_fin_done, 1)
            pool.wait_ge(stored, 16 * (CHUNKS - 1))

        @block.scalar
        def _(act):
            def split_w(c, j):
                count, per = came(j)
                act.wait_ge(w_in_sbuf[RING3[j]], at(c, 16 * per, 16 * count))
                act.wait_ge(proj_done, primed(c, N, j - 1))
                act.activation(w_split[:, j % 2, 0], w_raw[:, RING3[j]], ACT.Copy).then_inc(w_hi, 1)

            junk = y_out[:, :, :].rearrange("p a t -> p (a t)")
            last_junk = kq_raw[:, :, :].rearrange("p a t -> p (a t)")

            def square(src, dst, before, junk=junk):
                if not (isinstance(before, int) and before == 0):
                    act.wait_ge(squared, before)
                act.activation(junk[:, 0:src.shape[1]], src, ACT.Square, accum_out=dst).then_inc(squared, 1)


            def turn_x(c, k):
                act.wait_ge(x_turned, at(c, KT, k + 1))
                act.activation(xn_hi[:, k], turn_bank(c, k), ACT.Copy, scale=g_in[:, k:k + 1])\
                    .then_inc(xn_hi_done, 1)

            def copy_out(c, edge, j):
                kind, n = ITEMS[j]
                if kind not in "KVQHOGA":
                    return
                act.wait_ge(proj_done, primed(c, N, j + 1))
                src = ps_proj[RING3[j]]
                if kind in "KVQ":
                    turn = KQV.index((kind, n)) % 2
                    if (kind, n) == ("Q", 1):
                        act.wait_ge(v_turned, at(c, 1, 1))
                    act.activation(kq_raw[:, turn], src[:, :], ACT.Copy).then_inc(copied, 1)
                elif kind == "H":
                    act.activation(h_in[:, :], src[:, :], ACT.Copy).then_inc(copied, 1)
                elif kind == "O":
                    if n == 0:
                        act.wait_ge(squared, LAST_SQUARES if edge else squares(c, True, 0))
                    if n >= 2:
                        act.wait_ge(y_turned, at(c, KT, n - 1))
                    act.activation(y_out[:, n % 2], src[:, :], ACT.Copy).then_inc(copied, 1)
                else:
                    act.activation(th[:, :], src[:, :], ACT.Tanh, scale=0.5).then_inc(tanh_done, 1)

            def high_part(c, j):
                kind, n = ITEMS[j]
                if kind in "KQ":
                    i = ROPED.index((kind, n))
                    act.wait_ge(rope_step, primed(c, STEPS_ROPE * len(ROPED), STEPS_ROPE * (i + 1)))
                if kind == "K":
                    act.activation(k_st[:, :, 0:P], k_st[:, :, T:T + P].bitcast(F32), ACT.Copy)\
                        .then_inc(kept, 1)
                    act.wait_ge(kept, at(c, 2, 1))
                    for kv in range(N_KV_HEADS):
                        src = rot_a[kv * HEAD_DIM:(kv + 1) * HEAD_DIM, :]
                        for half in range(2):
                            ins = act.activation(k_st[half * HEAD_DIM:(half + 1) * HEAD_DIM, 2 * kv, P:],
                                                 src, ACT.Copy)
                    ins.then_inc(kq_hi, 1)
                elif kind == "Q":
                    act.activation(q_st[0:HEAD_DIM, 2 * n], rot_a[0:HEAD_DIM, :], ACT.Copy)
                    act.activation(q_st[HEAD_DIM:P, 2 * n + 1], rot_a[HEAD_DIM:P, :], ACT.Copy)\
                        .then_inc(kq_hi, 1)
                elif kind in "BA":
                    act.wait_ge(made, primed(c, len(MADE), MADE.index((kind, n)) + 1))
                    act.activation(mix_hi[:, MIX_TILE[kind, n]], y[:, :], ACT.Copy, scale=0.5)\
                        .then_inc(mix_hi_done, 1)

            def v_high(c):
                act.wait_ge(v_turned, at(c, 1, 1))
                act.activation(v_st[:, 0], v_st[:, BLOCKS].bitcast(F32), ACT.Copy).then_inc(kept, 1)
                act.wait_ge(kept, at(c, 2, 2))
                act.activation(v_st[:, 1:, :, 0, :],
                               ps_o[:, :].rearrange("p (b k d) -> p b k d", b=BLOCKS, k=N_KV_HEADS),
                               ACT.Copy).then_inc(v_hi, 1)

            def exps(c, un):
                for i in range(GROUP):
                    act.wait_ge(max_done, at(c, UNITS * GROUP, un * GROUP + i + 1))
                    act.activation(probs[:, i], probs[:, i], ACT.Exp, bias=neg_max[:, i:i + 1],
                                   scale=-1.0, accum_out=row_sum[:, i:i + 1])
                act.wait_ge(off_done, at(c, UNITS, un + 1))
                act.activation(sink_exp[:, :], sink_off[:, :], ACT.Exp).then_inc(exp_done, 1)

            def probs_high(c, un):
                for kb in range(2):
                    act.wait_ge(p_turned, at(c, 2 * UNITS, 2 * un + kb + 1))
                    act.activation(pt_hi[:, kb], ps_t[:, kb], ACT.Copy).then_inc(pt_hi_done, 1)

            def copy_o(c, un):
                g, b = divmod(un, BLOCKS)
                pair = slice(g * GROUP // 2, (g + 1) * GROUP // 2)
                o = ps_o[:, :].rearrange("p (i e q) -> p i e q", i=GROUP // 2, e=2)
                act.wait_ge(pv_done, at(c, UNITS, un + 1))
                act.activation(attn[HEAD_DIM:P, pair, b * P:(b + 1) * P], o[0:HEAD_DIM, :, 1], ACT.Copy)
                act.activation(attn[0:HEAD_DIM, pair, b * P:(b + 1) * P], o[HEAD_DIM:P, :, 0], ACT.Copy)\
                    .then_inc(o_copied, 1)

            act.sem_inc(copied, len(FROM_ACT))
            for t in range(BLOCKS):
                act.wait_ge(x_first[t], 16)
                square(x_next[:, t], sq_in[:, t:t + 1], t)
            split_w(0, 0)
            act.wait_ge(rows_turned, 1)
            act.activation(vecs[:, :], ps_o[:, 0:KT + CONV_K * CONVS], ACT.Copy).then_inc(vecs_done, 1)
            act.wait_ge(vecs_done, 1)
            for k in range(KT):
                turn_x(0, k)

            def result_sums(c, t):
                if t == 0:
                    act.wait_ge(h_added, primed(c, KT, KT))
                square(h[:, t], sq_fin[:, t:t + 1], squares(c, True, t))

            def slots(c, these, edge):
                for s in these:
                    if s + 1 == N and not edge:
                        split_w(c + 1, 0)
                    elif s + 1 < N and s != N_IN:
                        split_w(c, s + 1)
                    if s == 0 and not edge:
                        copy_out(c - 1, False, N - 1)
                    if s >= 2 and s != N_IN + 1:
                        high_part(c, s - 2)
                    if s >= 1:
                        copy_out(c, edge, s - 1)
                    if s == N_IN:
                        high_part(c, s - 1)
                        split_w(c, s + 1)
                    if s == V_TURN:
                        v_high(c)
                    if s in TURN_SLOT:
                        probs_high(c, TURN_SLOT.index(s))
                    if s in PV_SLOT:
                        copy_o(c, PV_SLOT.index(s))
                    if s in QK_SLOT:
                        exps(c, QK_SLOT.index(s))
                    if not edge and s in RESULT_SLOT:
                        for t in range(BLOCKS):
                            if RESULT_SLOT[t] == s:
                                result_sums(c - 1, t)
                    if not edge and s in SQUARE_SLOT:
                        t = SQUARE_SLOT.index(s)
                        if t == 0:
                            act.wait_ge(x_in, at(c + 1, 16, 0))
                        square(x_next[:, t], sq_in[:, t:t + 1], squares(c, False, t))
                    if not edge and s in SCALE_SLOT:
                        t = SCALE_SLOT.index(s)
                        if t == 0:
                            act.wait_ge(r_in_done, at(c + 1, 1, BLOCKS))
                        act.activation(x_next[:, t], x_next[:, t], ACT.Copy, scale=r_in[:, t:t + 1])\
                            .then_inc(x_scaled, 1)
                    if not edge and N_IN <= s < N_IN + KT // 2:
                        turn_x(c + 1, 2 * (s - N_IN))
                        turn_x(c + 1, 2 * (s - N_IN) + 1)

            by_chunk(act, slots)
            cut = LAST_PART * P
            act.wait_ge(h_added, primed(CHUNKS - 1, KT, LAST_PART))
            for t in range(BLOCKS):
                square(h[:, t, 0:cut], sq_fin[:, t:t + 1], LAST_SQUARES + t, last_junk)
            copy_out(CHUNKS - 1, True, N - 1)
            act.wait_ge(h_added, primed(CHUNKS - 1, KT, KT))
            for t in range(BLOCKS):
                square(h[:, t, cut:], sq_rest[:, t:t + 1], LAST_SQUARES + BLOCKS + t, last_junk)
            act.wait_ge(r_fin_done, CHUNKS)
            act.wait_ge(gained, KT)
            for t in range(1, BLOCKS, 2):
                act.activation(x_next[:, t], x_next[:, t], ACT.Copy, scale=r_fin[:, t:t + 1])\
                    .then_inc(last_scaled[1], 1)

        @block.vector
        def _(dve):
            def split_w(c, j):
                dve.wait_ge(w_hi, at(c, N, j + 1))
                dve.tensor_tensor(w_split[:, j % 2, 1], w_raw[:, RING3[j]],
                                  w_split[:, j % 2, 0].bitcast(F32), ALU.subtract).then_inc(w_lo, 1)

            def scale_first_x(t):
                dve.wait_ge(r_in_done, t + 1)
                dve.tensor_scalar(x_next[:, t], x_next[:, t], r_in[:, t:t + 1], None, ALU.mult)\
                    .then_inc(x_scaled, 1)

            def turn_x(c, k):
                dve.wait_ge(xn_hi_done, at(c, KT, k + 1))
                dve.scalar_tensor_tensor(xn_lo[:, k], turn_bank(c, k), g_in[:, k:k + 1],
                                         xn_hi[:, k].bitcast(F32), ALU.mult, ALU.subtract)\
                    .then_inc(xn_lo_done, 1)

            def rotate(c, j):
                kind, n = ITEMS[j]
                i = ROPED.index((kind, n))
                turn = KQV.index((kind, n)) % 2
                done = STEPS_ROPE * i
                per = STEPS_ROPE * len(ROPED)
                src = kq_raw[:, turn]
                if i == 0:
                    dve.wait_ge(rope_in, at(c, 16, 16))
                dve.wait_ge(copied, primed(c, len(FROM_ACT), FROM_ACT.index((kind, n)) + 1))
                dve.wait_ge(kq_lo, primed(c, len(ROPED), i))
                half = ROT_DIM // 2
                swap = [p ^ half if p < ROT_DIM else p for p in range(32)]
                dve.tensor_tensor(rot_a[:, :], src, rope_t[:, 0], ALU.mult).then_inc(rope_step, 1)
                dve.stream_shuffle(rot_b[:, :], src, swap).then_inc(rope_step, 1)
                dve.wait_ge(rope_step, primed(c, per, done + 2))
                dve.tensor_tensor(rot_b[:, :], rot_b[:, :], rope_t[:, 1], ALU.mult).then_inc(rope_step, 1)
                dve.wait_ge(rope_step, primed(c, per, done + 3))
                dve.tensor_tensor(rot_a[:, :], rot_a[:, :], rot_b[:, :], ALU.add).then_inc(rope_step, 1)

            def y_free(c, item):
                dve.wait_ge(mix_lo_done, primed(c, len(MADE), MADE.index(item)))

            def convolve(c, n):
                per, done = STEPS_CONV * CONVS, STEPS_CONV * n
                bank = ps_proj[RING3[ITEMS.index(("C", n))]]
                lag = CONV_K - 1
                dve.wait_ge(proj_done, primed(c, N, ITEMS.index(("C", n)) + 1))
                dve.wait_ge(copied, primed(c, len(FROM_ACT), FROM_ACT.index(("H", n)) + 1))
                dve.wait_ge(conv_step, primed(c, per, done))
                dve.tensor_copy(u[:, 0:lag], u_tail[:, n]).then_inc(conv_step, 1)
                dve.tensor_tensor(u[:, lag:], bank[:, :], h_in[:, :], ALU.mult).then_inc(conv_step, 1)
                dve.wait_ge(conv_step, primed(c, per, done + 2))
                y_free(c, ("B", n))
                dve.tensor_scalar(y[:, :], u[:, 0:T], taps[:, 0, n:n + 1], None, ALU.mult)\
                    .then_inc(conv_step, 1)
                for j in range(1, CONV_K):
                    dve.wait_ge(conv_step, primed(c, per, done + 2 + j))
                    dve.scalar_tensor_tensor(y[:, :], u[:, j:j + T], taps[:, j, n:n + 1], y[:, :],
                                             ALU.mult, ALU.add).then_inc(conv_step, 1)
                dve.tensor_copy(u_tail[:, n], u[:, T:T + lag]).then_inc(conv_step, 1)

            def gate(c, j):
                kind, n = ITEMS[j]
                i = GATES.index((kind, n))
                dve.wait_ge(tanh_done, at(c, len(GATES), i + 1))
                dve.scalar_tensor_tensor(th[:, :], th[:, :], 1.0, ps_proj[RING3[j]][:, :],
                                         ALU.add, ALU.mult).then_inc(silu_done, 1)
                if kind == "A":
                    dve.wait_ge(o_added, primed(c, UNITS, BLOCKS * (n // (GROUP // 2) + 1)))
                    dve.wait_ge(silu_done, primed(c, len(GATES), i + 1))
                    y_free(c, (kind, n))
                    dve.tensor_tensor(y[:, :], th[:, :], attn[:, n], ALU.mult).then_inc(made, 1)
                else:
                    dve.wait_ge(conv_step, primed(c, STEPS_CONV * CONVS, STEPS_CONV * n + 5))
                    dve.wait_ge(silu_done, primed(c, len(GATES), i + 1))
                    dve.tensor_tensor(y[:, :], th[:, :], y[:, :], ALU.mult).then_inc(gated, 1)

            def times_b(c, j):
                n = ITEMS[j][1]
                dve.wait_ge(proj_done, primed(c, N, j + 1))
                dve.wait_ge(gated, at(c, CONVS, n + 1))
                dve.tensor_tensor(y[:, :], ps_proj[RING3[j]][:, :], y[:, :], ALU.mult).then_inc(made, 1)

            def add_h(c, m):
                if m == 0:
                    dve.wait_ge(h_in_sbuf, at(c, 16, 16))
                dve.wait_ge(y_turned, at(c, KT, m + 1))
                dst = h[:, :, m * P:(m + 1) * P]
                dve.tensor_tensor(dst, ps_s[:, m % 2].rearrange("p (t d) -> p t d", t=BLOCKS), dst,
                                  ALU.add).then_inc(h_added, 1)

            def low_part(c, j):
                kind, n = ITEMS[j]
                lo, hi = slice(0, HEAD_DIM), slice(HEAD_DIM, P)
                if kind in "KQ":
                    dve.wait_ge(kq_hi, at(c, len(ROPED), ROPED.index((kind, n)) + 1))
                if kind == "K":
                    for kv, own in enumerate((lo, hi)):
                        for half in (lo, hi):
                            ins = dve.tensor_tensor(k_st[half, 2 * kv + 1, P:], rot_a[own, :],
                                                    k_st[own, 2 * kv, P:].bitcast(F32), ALU.subtract)
                    ins.then_inc(kq_lo, 1)
                elif kind == "Q":
                    dve.tensor_tensor(q_st[hi, 2 * n], rot_a[lo, :], q_st[lo, 2 * n].bitcast(F32),
                                      ALU.subtract)
                    dve.tensor_tensor(q_st[lo, 2 * n + 1], rot_a[hi, :], q_st[hi, 2 * n + 1].bitcast(F32),
                                      ALU.subtract).then_inc(kq_lo, 1)
                elif kind in "BA":
                    k = MIX_TILE[kind, n]
                    dve.wait_ge(mix_hi_done, at(c, len(MADE), MADE.index((kind, n)) + 1))
                    dve.scalar_tensor_tensor(mix_lo[:, k], y[:, :], 0.5, mix_hi[:, k].bitcast(F32),
                                             ALU.mult, ALU.subtract).then_inc(mix_lo_done, 1)

            def v_low(c):
                dve.wait_ge(v_hi, at(c, 1, 1))
                dve.tensor_tensor(v_st[:, 1:, :, 1, :],
                                  ps_o[:, :].rearrange("p (b k d) -> p b k d", b=BLOCKS, k=N_KV_HEADS),
                                  v_st[:, 1:, :, 0, :].bitcast(F32), ALU.subtract).then_inc(v_lo, 1)

            def maxima(c, un):
                g, b = divmod(un, BLOCKS)
                mask = band_0 if b == 0 else band
                if un == 0:
                    wait_alone(dve, band_done, primed(c, 1, 0), dve_passed)
                wait_alone(dve, qk_done, at(c, UNITS, un + 1), dve_passed)
                for i in range(GROUP):
                    head = g * GROUP + i
                    dve.tensor_tensor_reduce(
                        out=probs[:, i], in0=ps_s[:, i // 2, (i % 2) * 2 * P:(i % 2 + 1) * 2 * P],
                        in1=mask[:, :], scale=-SCALE, scalar=neg_sink[:, head:head + 1],
                        op0=ALU.add, op1=ALU.min, accum_out=neg_max[:, i:i + 1]).then_inc(max_done, 1)
                dve.wait_ge(max_done, at(c, UNITS * GROUP, (un + 1) * GROUP))
                dve.tensor_tensor(sink_off[:, :], neg_max[:, :], sink[:, g * GROUP:(g + 1) * GROUP],
                                  ALU.add).then_inc(off_done, 1)

            def normalize(c, un):
                dve.wait_ge(exp_done, at(c, UNITS, un + 1))
                dve.tensor_tensor(denom[:, :], row_sum[:, :], sink_exp[:, :], ALU.add)\
                    .then_inc(norm_step, 1)
                dve.wait_ge(norm_step, at(c, 2 * UNITS, 2 * un + 1))
                dve.reciprocal(inv[:, :], denom[:, :]).then_inc(norm_step, 1)
                dve.wait_ge(norm_step, at(c, 2 * UNITS, 2 * un + 2))
                for i in range(GROUP):
                    ins = dve.tensor_scalar(probs[:, i], probs[:, i], inv[:, i:i + 1], None, ALU.mult)
                ins.then_inc(p_ready, 1)

            def probs_low(c, un):
                for kb in range(2):
                    dve.wait_ge(pt_hi_done, at(c, 2 * UNITS, 2 * un + kb + 1))
                    dve.tensor_tensor(pt_lo[:, kb], ps_t[:, kb], pt_hi[:, kb].bitcast(F32),
                                      ALU.subtract).then_inc(pt_lo_done, 1)

            def add_o(c, un):
                g, b = divmod(un, BLOCKS)
                pair = slice(g * GROUP // 2, (g + 1) * GROUP // 2)
                o = ps_o[:, :].rearrange("p (i e q) -> p i e q", i=GROUP // 2, e=2)
                dve.wait_ge(o_copied, at(c, UNITS, un + 1))
                for e, half in enumerate((slice(0, HEAD_DIM), slice(HEAD_DIM, P))):
                    dst = attn[half, pair, b * P:(b + 1) * P]
                    ins = dve.tensor_tensor(dst, o[half, :, e], dst, ALU.add)
                ins.then_inc(o_added, 1)

            for primed_sem, per in ((w_lo, N), (rope_step, STEPS_ROPE * len(ROPED)),
                                    (conv_step, STEPS_CONV * CONVS), (silu_done, len(GATES)),
                                    (made, len(MADE)), (o_added, UNITS), (h_added, KT),
                                    (kq_lo, len(ROPED)), (mix_lo_done, len(MADE))):
                dve.sem_inc(primed_sem, per)
            dve.memset(k_st[:, :, T:T + P].bitcast(F32), 0.0)
            dve.memset(v_st[:, BLOCKS].bitcast(F32), 0.0).then_inc(signs, 1)
            for t in range(BLOCKS):
                scale_first_x(t)
            split_w(0, 0)
            dve.wait_ge(vecs_done, 1)
            for k in range(KT):
                turn_x(0, k)
            dve.wait_ge(consts_in, 32)
            dve.tensor_scalar(neg_sink[:, :], sink[:, :], -1.0, None, ALU.mult).then_inc(signs, 1)
            dve.wait_ge(signs, 2)
            dve.wait_ge(consts_made, 9)

            def slots(c, these, edge):
                for s in these:
                    if s + 1 == N and not edge:
                        split_w(c + 1, 0)
                    elif s + 1 < N and s != N_IN:
                        split_w(c, s + 1)
                    if s < 2 and not edge:
                        add_h(c - 1, KT - 2 + s)
                    if s - 1 in QK_SLOT:
                        normalize(c, QK_SLOT.index(s - 1))
                    if s in TURN_SLOT:
                        probs_low(c, TURN_SLOT.index(s))
                    if s in QK_SLOT:
                        maxima(c, QK_SLOT.index(s))
                    if s in PV_SLOT:
                        add_o(c, PV_SLOT.index(s))
                    if s >= 2 and s != N_IN + 1:
                        low_part(c, s - 2)
                    if s >= 1:
                        kind, n = ITEMS[s - 1]
                        if kind in "KQ":
                            rotate(c, s - 1)
                        elif kind == "C":
                            convolve(c, n)
                        elif kind in "GA":
                            gate(c, s - 1)
                        elif kind == "B":
                            times_b(c, s - 1)
                    if s == N_IN:
                        low_part(c, s - 1)
                        split_w(c, s + 1)
                    if s == V_TURN:
                        v_low(c)
                    if s in FINISH_SLOT and not edge:
                        for t in range(BLOCKS):
                            if FINISH_SLOT[t] == s:
                                if t == 0:
                                    dve.wait_ge(r_fin_done, at(c - 1, 1, 1))
                                dve.scalar_tensor_tensor(h[:, t], h[:, t], r_fin[:, t:t + 1], g_fin[:, :],
                                                         ALU.mult, ALU.mult).then_inc(finished, 1)
                    if not edge and N_IN <= s < N_IN + KT // 2:
                        turn_x(c + 1, 2 * (s - N_IN))
                        turn_x(c + 1, 2 * (s - N_IN) + 1)
                    if s > N_IN + 1:
                        add_h(c, s - N_IN - 2)
                        if edge:
                            gain(s - N_IN - 2)

            def gain(m):
                dve.wait_ge(h_added, primed(CHUNKS - 1, KT, m + 1))
                cols = slice(m * P, (m + 1) * P)
                dve.tensor_tensor(x_next[:, :, cols], h[:, :, cols],
                                  g_fin[:, None, cols].broadcast_to([P, BLOCKS, P]), ALU.mult)\
                    .then_inc(gained, 1)

            by_chunk(dve, slots)
            for m in (KT - 2, KT - 1):
                add_h(CHUNKS - 1, m)
                gain(m)
            dve.wait_ge(squared, LAST_SQUARES + BLOCKS)
            dve.tensor_scalar(mean_fin[:, :], sq_fin[:, :], 1.0 / D_MODEL, EPS, ALU.mult, ALU.add)\
                .then_inc(last_mean_done, 1)
            dve.wait_ge(squared, LAST_SQUARES + 2 * BLOCKS)
            dve.wait_ge(last_mean_done, 1)
            dve.scalar_tensor_tensor(mean_fin[:, :], sq_rest[:, :], 1.0 / D_MODEL, mean_fin[:, :],
                                     ALU.mult, ALU.add).then_inc(last_mean_done, 1)
            dve.wait_ge(r_fin_done, CHUNKS)
            dve.wait_ge(gained, KT)
            for t in range(0, BLOCKS, 2):
                dve.tensor_scalar(x_next[:, t], x_next[:, t], r_fin[:, t:t + 1], None, ALU.mult)\
                    .then_inc(last_scaled[0], 1)

        @block.tensor
        def _(pe):
            def product(c, j):
                kind, n = ITEMS[j]
                i, back = before(j)
                pe.wait_ge(w_lo, primed(c, N, j + 1))
                bank_free, per, k = released(i)
                pe.wait_ge(bank_free, primed(c, per, k - per * back))
                hi, lo = (mix_hi, mix_lo) if kind == "O" else (xn_hi, xn_lo)
                order = [MIX_TILE[i] for i in MADE] if kind == "O" else range(KT)
                for a, k in enumerate(order):
                    if j == 0:
                        pe.wait_ge(xn_lo_done, at(c, KT, k + 1))
                    if kind == "O" and n == 0:
                        pe.wait_ge(mix_lo_done, primed(c, len(MADE), a + 1))
                    for b, (w, v) in enumerate(((0, hi), (0, lo), (1, hi))):
                        mm = pe.matmul(ps_proj[RING3[j]][:, :], w_split[:, j % 2, w, k], v[:, k],
                                       start=a == 0 and b == 0, stop=a == KT - 1 and b == 2)
                    if isinstance(c, int) and c == 0 and j == 0 and a < KT - 4:
                        turn_x(0, a + 4)
                mm.then_inc(proj_done, 1)

            def turn_v(c):
                pe.wait_ge(copied, primed(c, len(FROM_ACT), FROM_ACT.index(("V", 0)) + 1))
                pe.wait_ge(o_added, primed(c, UNITS, 0))
                for b in range(BLOCKS):
                    mm = pe.transpose(ps_o[:, b * P:(b + 1) * P], kq_raw[:, 1, b * P:(b + 1) * P], ident[:, :])
                mm.then_inc(v_turned, 1)

            def scores(c, un):
                g, b = divmod(un, BLOCKS)
                pe.wait_ge(kq_lo, primed(c, len(ROPED), 1 + (g + 1) * GROUP // 2))
                if un == 0:
                    pe.wait_ge(h_added, primed(c, KT, 0))
                for i in range(GROUP):
                    for part in range(2):
                        mm = pe.matmul(ps_s[:, i // 2, (i % 2) * 2 * P:(i % 2 + 1) * 2 * P],
                                       q_st[:, g * GROUP + i, b * P:(b + 1) * P],
                                       k_st[:, 2 * g + part, b * P:(b + 2) * P],
                                       start=part == 0, stop=part == 1)
                mm.then_inc(qk_done, 1)

            def turn_p(c, un):
                pe.wait_ge(p_ready, at(c, UNITS, un + 1))
                for kb in range(2):
                    for i in range(GROUP):
                        mm = pe.transpose(ps_t[:, kb, i * P:(i + 1) * P], probs[:, i, kb * P:(kb + 1) * P],
                                          ident[:, :])
                    mm.then_inc(p_turned, 1)

            def values(c, un):
                g, b = divmod(un, BLOCKS)
                if un == 0:
                    pe.wait_ge(v_lo, at(c, 1, 1))
                else:
                    pe.wait_ge(o_added, primed(c, UNITS, un))
                for kb in range(2):
                    pe.wait_ge(pt_lo_done, at(c, 2 * UNITS, 2 * un + kb + 1))
                    for part, pt in enumerate((pt_hi, pt_lo)):
                        mm = pe.matmul(ps_o[:, :],
                                       v_st[:, b + kb, g].rearrange("p a d -> p (a d)"), pt[:, kb],
                                       start=kb == 0 and part == 0, stop=kb == 1 and part == 1)
                mm.then_inc(pv_done, 1)

            def turn_x(c, k):
                if k == 0:
                    pe.wait_ge(x_scaled, at(c, BLOCKS, BLOCKS))
                banks = 4 if isinstance(c, int) and c == 0 else 2
                if k >= banks:
                    pe.wait_ge(xn_lo_done, at(c, KT, k - banks + 1))
                for t in range(BLOCKS):
                    mm = pe.transpose(turn_bank(c, k)[:, t * P:(t + 1) * P], x_next[:, t, k * P:(k + 1) * P],
                                      ident[:, :])
                mm.then_inc(x_turned, 1)

            def turn_y(c, m):
                pe.wait_ge(copied, primed(c, len(FROM_ACT), FROM_ACT.index(("O", m)) + 1))
                if m >= 2:
                    pe.wait_ge(h_added, primed(c, KT, m - 1))
                for t in range(BLOCKS):
                    mm = pe.transpose(ps_s[:, m % 2, t * P:(t + 1) * P], y_out[:, m % 2, t * P:(t + 1) * P],
                                      ident[:, :])
                mm.then_inc(y_turned, 1)

            pe.sem_inc(proj_done, N)
            pe.wait_ge(consts_made, 7)
            pe.wait_ge(rows_in, 32)
            pe.transpose(ps_o[:, 0:KT + CONV_K * CONVS], vec_rows[:, :],
                         ident[0:KT + CONV_K * CONVS, 0:KT + CONV_K * CONVS]).then_inc(rows_turned, 1)
            for k in range(4):
                turn_x(0, k)

            def slots(c, these, edge):
                for s in these:
                    if s == 1 and not edge:
                        turn_y(c - 1, KT - 1)
                    if s == V_TURN:
                        turn_v(c)
                    if s in PV_SLOT:
                        values(c, PV_SLOT.index(s))
                    if s in TURN_SLOT:
                        turn_p(c, TURN_SLOT.index(s))
                    if s in QK_SLOT:
                        scores(c, QK_SLOT.index(s))
                    if not edge and N_IN <= s < N_IN + KT // 2:
                        turn_x(c + 1, 2 * (s - N_IN))
                        turn_x(c + 1, 2 * (s - N_IN) + 1)
                    product(c, s)
                    if s > N_IN:
                        turn_y(c, s - N_IN - 1)

            by_chunk(pe, slots)
            turn_y(CHUNKS - 1, KT - 1)


_INS = ["x", "norm_g", "w_in", "sinks", "conv_w", "w_out", "final_g"]


def rope_tables():
    import numpy as np
    half = ROT_DIM // 2
    inv_freq = np.float32(500000.0) ** (-np.arange(0, ROT_DIM, 2, dtype=np.float32) / np.float32(ROT_DIM))
    ang = np.arange(SEQ, dtype=np.float32)[None, :] * inv_freq.astype(np.float32)[:, None]
    cos, sin = np.cos(ang.astype(np.float64)), np.sin(ang.astype(np.float64))
    table = np.zeros((2, HEAD_DIM, SEQ), np.float64)
    table[0] = 1.0
    table[0, :ROT_DIM] = np.concatenate([cos, cos])
    table[1, :ROT_DIM] = np.concatenate([-sin, sin])
    table = np.concatenate([table] * (P // HEAD_DIM), axis=1).reshape(2, P, CHUNKS, T)
    return np.ascontiguousarray(table.transpose(1, 2, 0, 3).astype(np.float32))


def kernel(**inputs):
    import numpy as np
    import concourse.bacc as bacc
    from concourse.bass_utils import run_bass_kernel_spmd

    nc = bacc.Bacc("TRN2", target_bir_lowering=False, num_devices=1)
    arrays, args = {}, []
    for name, a in [(n, inputs[n]) for n in _INS] + [("rope", rope_tables())]:
        a = np.ascontiguousarray(a)
        arrays[f"in_{name}"] = a
        args.append(nc.dram_tensor(f"in_{name}", a.shape, mybir.dt.from_np(a.dtype), kind="ExternalInput").ap())
    args.append(nc.dram_tensor("out_0", (1, SEQ, D_MODEL), F32, kind="ExternalOutput").ap())
    hybrid_layer(nc, *args)
    r = run_bass_kernel_spmd(nc, [arrays], core_ids=[0])
    return r.results[0]["out_0"]
```

```python
from contextlib import ExitStack

import concourse.bass as bass
from concourse import mybir

ALU = mybir.AluOpType
ACT = mybir.ActivationFunctionType
F32 = mybir.dt.float32
F32R = mybir.dt.float32r

P = 128
D_MODEL = 1024
SEQ = 2048
HEAD_DIM = 64
N_Q_HEADS = 8
N_KV_HEADS = 2
GROUP = N_Q_HEADS // N_KV_HEADS
CONV_K = 3
ROT_DIM = HEAD_DIM // 4
EPS = 1e-5
SCALE = HEAD_DIM ** -0.5
MASKED = -3.0e38

T = 512
CHUNKS = SEQ // T
BLOCKS = T // P
KT = D_MODEL // P
PAIRS = N_Q_HEADS // 2
CONVS = 4
UNITS = N_KV_HEADS * BLOCKS

COL = {"Q": 0, "K": 4, "V": 5, "A": 6, "B": 10, "C": 14, "H": 18, "G": 22}
ITEMS = [("K", 0), ("V", 0), ("Q", 0), ("Q", 1),
         ("H", 0), ("C", 0), ("G", 0), ("B", 0),
         ("Q", 2), ("Q", 3),
         ("H", 1), ("C", 1), ("G", 1), ("B", 1),
         ("H", 2), ("C", 2), ("G", 2), ("B", 2),
         ("A", 0), ("A", 1),
         ("H", 3), ("C", 3), ("G", 3),
         ("A", 2), ("A", 3), ("B", 3)] + [("O", m) for m in range(KT)]
N = len(ITEMS)
N_IN = N - KT
RING3 = [j % 3 for j in range(N - 1)] + [1]
MADE = [i for i in ITEMS if i[0] in "BA"]
MIX_TILE = {i: (i[1] if i[0] == "A" else PAIRS + i[1]) for i in MADE}
GATES = [i for i in ITEMS if i[0] in "GA"]
ROPED = [i for i in ITEMS if i[0] in "KQ"]
KQV = [i for i in ITEMS if i[0] in "KQV"]
FROM_ACT = [i for i in ITEMS if i[0] in "KVQHGA"]

V_TURN = 3
HEAD = 10
QK_SLOT = [7 + 2 * u for u in range(UNITS)]
TURN_SLOT = [s + 2 for s in QK_SLOT]
PV_SLOT = [s + 3 for s in QK_SLOT]
STORE_SLOT, RELOAD_SLOT = HEAD - 1, HEAD + 3
SQUARE_SLOT = [14 + k for k in range(KT)]
SUM_SLOT, SPREAD_SLOT, COPY_SLOT = 23, 25, N_IN + 1
HIGH_SLOT = [N_IN] + [N_IN + k for k in range(KT - 1)]
LOW_SLOT = [s + 1 for s in HIGH_SLOT]
R_SUM_SLOT, R_SPREAD_SLOT = 2, 4
FINISH_SLOT = [5, 5, 6, 6, 7, 7, 8, 8]

TURN_AT, PV_AT, SUM_AT, LAST_SUM_AT = 1, 5, 5, 4

WARM_UP = 12
BETWEEN = 4

STEPS_ROPE = 4
STEPS_CONV = 6
STEPS_H = 2
STEPS_TRIANGLE = 4


def at(c, per, k):
    return c * per + k


def primed(c, per, k):
    return c * per + per + k


def wait_alone(eng, sem, value, passed):
    eng.wait_ge(sem, value)
    eng.sem_inc(passed, 1)


def before(j):
    for back in (0, 1):
        for i in range(j - 1 if not back else N - 1, -1, -1):
            if RING3[i] == RING3[j]:
                return i, back


def hybrid_layer(nc, x_t, g_in_t, w_items, sinks, taps_t, g_fin_t, rope, out_t):
    with ExitStack() as ctx:
        def sb(name, shape, dt=F32):
            return ctx.enter_context(nc.sbuf_tensor(name, shape, dt))

        def ps(name, shape):
            return ctx.enter_context(nc.psum_tensor(name, shape, F32))

        def sem(name):
            return ctx.enter_context(nc.semaphore(name))

        w_raw = sb("w_raw", [P, 3, KT, P])
        w_split = sb("w_split", [P, 2, 2, KT, P], F32R)
        xn_hi = sb("xn_hi", [P, KT, T], F32R)
        xn_lo = sb("xn_lo", [P, KT, T], F32R)
        mix_hi = sb("mix_hi", [P, KT, T], F32R)
        mix_lo = sb("mix_lo", [P, KT, T], F32R)
        x_next = sb("x_next", [P, KT, T])
        h = sb("h", [P, KT, T])
        q_st = sb("q_st", [P, N_Q_HEADS, T], F32R)
        k_st = sb("k_st", [P, 4, P + T], F32R)
        v_st = sb("v_st", [P, 1 + BLOCKS, N_KV_HEADS, 2, HEAD_DIM], F32R)
        rope_t = sb("rope_t", [P, 2, T])
        kq_raw = sb("kq_raw", [P, 2, T])
        rot_a = sb("rot_a", [P, T])
        rot_b = sb("rot_b", [P, T])
        probs = sb("probs", [P, GROUP, P])
        pt_hi = sb("pt_hi", [P, 2, GROUP, P], F32R)
        pt_lo = sb("pt_lo", [P, 2, GROUP, P], F32R)
        attn = sb("attn", [P, PAIRS, T])
        by_r = sb("by_r", [P, T])
        u = sb("u", [P, CONV_K - 1 + T])
        u_tail = sb("u_tail", [P, CONVS, CONV_K - 1])
        y = sb("y", [P, T])
        th = sb("th", [P, T])
        sq = sb("sq", [P, 2, T])
        acc = sb("acc", [P, T])
        r_all = sb("r_all", [P, T])
        ones = sb("ones", [P, 1])
        ident = sb("ident", [P, P])
        own = sb("own", [P, P], mybir.dt.int32)
        before_bias = sb("before_bias", [P, 1])
        g_in = sb("g_in", [P, KT])
        g_fin = sb("g_fin", [P, KT])
        taps = sb("taps", [P, CONV_K, CONVS])
        sink = sb("sink", [P, N_Q_HEADS])
        neg_sink = sb("neg_sink", [P, N_Q_HEADS])
        neg_max = sb("neg_max", [P, GROUP])
        score_max = sb("score_max", [P, GROUP])
        sink_off = sb("sink_off", [P, GROUP])
        sink_exp = sb("sink_exp", [P, GROUP])
        row_sum = sb("row_sum", [P, GROUP])
        denom = sb("denom", [P, GROUP])
        inv = sb("inv", [P, GROUP])
        mean = sb("mean", [P, BLOCKS])
        r = sb("r", [P, BLOCKS])
        minus_half = sb("minus_half", [P, BLOCKS])

        ps_proj = [ps(f"ps_proj{i}", [P, T]) for i in range(3)]
        ps_s = ps("ps_s", [P, 2, T])
        ps_t = ps("ps_t", [P, 2, T])
        ps_o = ps("ps_o", [P, T])

        w_in_sbuf = [sem(f"w_in_sbuf{i}") for i in range(3)]
        g_in_sbuf = sem("g_in_sbuf")
        consts_in = sem("consts_in")
        rope_in = sem("rope_in")
        x_first = [sem(f"x_first{t}") for t in range(KT)]
        x_in = sem("x_in")
        h_in_sbuf = sem("h_in_sbuf")
        stored = sem("stored")
        stored_last = sem("stored_last")
        proj_done = sem("proj_done")
        v_turned = sem("v_turned")
        qk_done = sem("qk_done")
        p_turned = sem("p_turned")
        pv_done = sem("pv_done")
        summed = sem("summed")
        spread = sem("spread")
        w_hi = sem("w_hi")
        copied = sem("copied")
        kq_hi = sem("kq_hi")
        v_hi = sem("v_hi")
        kept = sem("kept")
        before_copied = sem("before_copied")
        exp_done = sem("exp_done")
        p_ready = sem("p_ready")
        pt_hi_done = sem("pt_hi_done")
        o_copied = sem("o_copied")
        tanh_done = sem("tanh_done")
        mix_hi_done = sem("mix_hi_done")
        xn_hi_done = sem("xn_hi_done")
        r_copied = sem("r_copied")
        one_made = sem("one_made")
        squared = sem("squared")
        w_lo = sem("w_lo")
        rope_step = sem("rope_step")
        kq_lo = sem("kq_lo")
        v_lo = sem("v_lo")
        own_copied = sem("own_copied")
        scores_max = sem("scores_max")
        max_done = sem("max_done")
        off_done = sem("off_done")
        denom_done = sem("denom_done")
        inv_done = sem("inv_done")
        pt_lo_done = sem("pt_lo_done")
        o_added = sem("o_added")
        conv_step = sem("conv_step")
        silu_done = sem("silu_done")
        gated = sem("gated")
        made = sem("made")
        mix_lo_done = sem("mix_lo_done")
        xn_lo_done = sem("xn_lo_done")
        h_added = sem("h_added")
        finished = sem("finished")
        added_up = sem("added_up")
        mean_done = sem("mean_done")
        last_finished = sem("last_finished")
        signs = sem("signs")
        consts_made = sem("consts_made")
        pool_squared = sem("pool_squared")
        r_done = sem("r_done")
        rope_scaled = sem("rope_scaled")
        v_scaled = sem("v_scaled")
        h_scaled = sem("h_scaled")
        g_scaled = sem("g_scaled")
        y_scaled = sem("y_scaled")
        bias_done = sem("bias_done")
        triangle = sem("triangle")

        last_product = sem("last_product")
        last_added = sem("last_added")
        last_squared = sem("last_squared")
        last_summed = sem("last_summed")
        last_mean = sem("last_mean")
        last_r = sem("last_r")
        last_spread = sem("last_spread")

        pool_passed = sem("pool_passed")
        dve_passed = sem("dve_passed")

        def came(j):
            return RING3[:j + 1].count(RING3[j]), RING3.count(RING3[j])

        def released(j):
            kind, n = ITEMS[j]
            if kind == "O":
                return h_added, KT, n + 1
            if kind == "C":
                return conv_step, STEPS_CONV * CONVS, STEPS_CONV * n + 2
            if kind in "KVQHGA":
                return copied, len(FROM_ACT), FROM_ACT.index(ITEMS[j]) + 1
            return made, len(MADE), MADE.index(ITEMS[j]) + 1

        def made_in(item):
            return acc if item in (("A", 2), ("A", 3)) else y

        def norm_in(c):
            return 2 * c

        def norm_fin(c):
            return 2 * c + 3

        NORMS = 2 * CHUNKS
        HALVES = 2
        TOKENS = [slice(i * T // HALVES, (i + 1) * T // HALVES) for i in range(HALVES)]
        TILES = [slice(i * BLOCKS // HALVES, (i + 1) * BLOCKS // HALVES) for i in range(HALVES)]
        LAST_BANK = [ps_proj[RING3[N - 1]][:, :], ps_o[:, :]]
        LAST_R = [ps_t[:, 1], ps_t[:, 0]]
        BY_POOL = 4

        def by_chunk(eng, slots):
            slots(0, range(HEAD), True)
            with eng.Fori(0, CHUNKS - 1) as c:
                slots(c, range(HEAD, N), False)
                slots(c + 1, range(HEAD), False)
            slots(CHUNKS - 1, range(HEAD, N), True)

        block = ctx.enter_context(nc.Block())

        @block.sync
        def _(sp):
            def load_x_first(k):
                sp.dma_start(x_next[:, k], x_t[0, :, k]).then_inc(x_first[k], 16)

            sp.dma_start(g_in[:, :], g_in_t).then_inc(g_in_sbuf, 16)
            load_x_first(0)

            def slots(c, these, edge):
                for j in these:
                    i, back = before(j)
                    count, per = came(j)
                    sp.wait_ge(w_lo, primed(c, N, i + 1 - N * back))
                    sp.dma_start(w_raw[:, RING3[j]], w_items[j]).then_inc(w_in_sbuf[RING3[j]], 16)
                    if j == 0 and these.start == 0 and edge:
                        for k in range(1, KT):
                            load_x_first(k)
                    if j == 1:
                        sp.wait_ge(rope_step, primed(c, STEPS_ROPE * len(ROPED), 0))
                        sp.dma_start(rope_t[:, :, :], rope[:, bass.ds(c, 1)].rearrange("p o a t -> p (o a) t"))\
                            .then_inc(rope_in, 16)

            by_chunk(sp, slots)
            for half in range(HALVES):
                for n in range(0, KT, 2):
                    sp.wait_ge(last_finished, KT * half + n + 2)
                    sp.dma_start(out_t[CHUNKS - 1, :, n:n + 2, TOKENS[half]], h[:, n:n + 2, TOKENS[half]])\
                        .then_inc(stored_last, 16)
            sp.wait_ge(stored_last, 16 * HALVES * KT // 2)

        @block.gpsimd
        def _(pool):
            pool.memset(u_tail[:, :, :], 0.0).then_inc(consts_made, 1)
            pool.dma_start(sink[:, :], sinks.partition_broadcast(P)).then_inc(consts_in, 16)
            pool.dma_start(g_fin[:, :], g_fin_t).then_inc(stored, 16)
            pool.dma_start(taps[:, :, :], taps_t).then_inc(consts_in, 16)
            pool.memset(ident[:, :], 0.0).then_inc(consts_made, 1)
            pool.memset(minus_half[:, :], -0.5).then_inc(consts_made, 1)
            pool.memset(own[:, :], 1).then_inc(consts_made, 1)
            pool.wait_ge(consts_made, 4)
            pool.affine_select(out=ident[:, :], in_=ident[:, :], compare_op=ALU.not_equal, fill=1.0,
                               base=0, pattern=[[-1, P]], channel_multiplier=1).then_inc(consts_made, 1)
            pool.affine_select(out=own[:, :], in_=own[:, :], compare_op=ALU.is_ge, fill=0,
                               base=0, pattern=[[-1, P]], channel_multiplier=1).then_inc(consts_made, 1)
            pool.memset(before_bias[:, :], MASKED).then_inc(bias_done, 1)

            for k in range(BY_POOL):
                pool.wait_ge(x_first[k], 16)
                pool.tensor_tensor(attn[:, k], x_next[:, k], x_next[:, k], ALU.mult).then_inc(pool_squared, 1)
                if k:
                    pool.wait_ge(pool_squared, 2 * k)
                    pool.tensor_tensor(attn[:, 0], attn[:, 0], attn[:, k], ALU.add).then_inc(pool_squared, 1)

            def inverse_norm(number):
                wait_alone(pool, mean_done, number, pool_passed)
                pool.tensor_tensor(r[:, :], mean[:, :], minus_half[:, :], ALU.pow).then_inc(r_done, 1)

            def was_copied(c, j):
                wait_alone(pool, copied, primed(c, len(FROM_ACT), FROM_ACT.index(ITEMS[j]) + 1), pool_passed)

            def times_r(tile, done):
                pool.tensor_tensor(tile, tile, r_all[:, :], ALU.mult).then_inc(done, 1)

            def scale_rope(c):
                wait_alone(pool, rope_in, at(c, 16, 16), pool_passed)
                wait_alone(pool, r_copied, at(c, 1, 1), pool_passed)
                pool.tensor_tensor(rope_t[:, :, :], rope_t[:, :, :],
                                   r_all[:, None, :].broadcast_to([P, 2, T]), ALU.mult)\
                    .then_inc(rope_scaled, 1)

            def scale_h(c, j):
                was_copied(c, j)
                times_r(by_r[:, :], h_scaled)
                wait_alone(pool, h_scaled, at(c, STEPS_H * CONVS, STEPS_H * ITEMS[j][1] + 1), pool_passed)
                times_r(by_r[:, :], h_scaled)

            def triangles(c, un):
                per = STEPS_TRIANGLE * UNITS
                for i, (pt, ready) in enumerate(((pt_hi, pt_hi_done), (pt_lo, pt_lo_done))):
                    wait_alone(pool, ready, at(c, UNITS, un + 1), pool_passed)
                    pool.affine_select(out=pt[:, 0], in_=pt[:, 1].bitcast(F32), compare_op=ALU.is_ge, fill=0.0,
                                       base=-1, pattern=[[0, GROUP], [-1, P]], channel_multiplier=1)\
                        .then_inc(triangle, 1)
                wait_alone(pool, triangle, at(c, per, STEPS_TRIANGLE * un + 2), pool_passed)
                for pt in (pt_hi, pt_lo):
                    pool.affine_select(out=pt[:, 1], in_=pt[:, 1].bitcast(F32), compare_op=ALU.is_ge, fill=0.0,
                                       base=0, pattern=[[0, GROUP], [1, P]], channel_multiplier=-1)\
                        .then_inc(triangle, 1)

            def slots(c, these, edge):
                for s in these:
                    if s == 1:
                        if edge:
                            inverse_norm(1)
                        scale_rope(c)
                    if s >= 1:
                        kind, n = ITEMS[s - 1]
                        if kind == "V":
                            was_copied(c, s - 1)
                            times_r(kq_raw[:, 1], v_scaled)
                        elif kind == "H":
                            scale_h(c, s - 1)
                        elif kind in "GA":
                            was_copied(c, s - 1)
                            times_r(by_r[:, :], g_scaled)
                        elif kind == "C":
                            wait_alone(pool, conv_step, primed(c, STEPS_CONV * CONVS, STEPS_CONV * n + 5),
                                       pool_passed)
                            times_r(y[:, :], y_scaled)
                    if s in TURN_SLOT:
                        triangles(c, TURN_SLOT.index(s))
                    if s == R_SUM_SLOT and not edge:
                        inverse_norm(norm_fin(c - 1))
                    if s == HEAD and not edge:
                        wait_alone(pool, xn_lo_done, at(c, KT, KT), pool_passed)
                        pool.dma_start(x_next[:, :, :], x_t[bass.ds(c + 1, 1)].rearrange("c p k t -> p (c k) t"))\
                            .then_inc(x_in, 16)
                    if s == TURN_SLOT[BLOCKS] and not edge:
                        wait_alone(pool, before_copied, at(c, UNITS, BLOCKS + 1), pool_passed)
                        pool.memset(before_bias[:, :], 0.0).then_inc(bias_done, 1)
                    if s == SUM_SLOT and not edge:
                        inverse_norm(norm_in(c + 1))
                    if s == STORE_SLOT and not edge:
                        wait_alone(pool, finished, primed(c, KT, 0), pool_passed)
                        pool.dma_start(out_t[bass.ds(c - 1, 1)].rearrange("c p k t -> p (c k) t"), h[:, :, :])\
                            .then_inc(stored, 16)
                    if s == RELOAD_SLOT:
                        wait_alone(pool, stored, at(c, 16, 16), pool_passed)
                        pool.dma_start(h[:, :, :], x_t[bass.ds(c, 1)].rearrange("c p k t -> p (c k) t"))\
                            .then_inc(h_in_sbuf, 16)

            by_chunk(pool, slots)
            for half in range(HALVES):
                pool.wait_ge(last_mean, half + 1)
                pool.tensor_tensor(r[:, TILES[half]], mean[:, TILES[half]], minus_half[:, TILES[half]], ALU.pow)\
                    .then_inc(last_r, 1)
            pool.wait_ge(stored, 16 * CHUNKS)

        @block.scalar
        def _(act):
            def split_w(c, j):
                count, per = came(j)
                act.wait_ge(w_in_sbuf[RING3[j]], at(c, 16 * per, 16 * count))
                act.wait_ge(proj_done, primed(c, N, j - 1))
                act.activation(w_split[:, j % 2, 0], w_raw[:, RING3[j]], ACT.Copy).then_inc(w_hi, 1)

            def square(number, k, src):
                first = isinstance(number, int) and number == 1
                done = k - (BY_POOL if first else 0)
                if done >= 2:
                    act.wait_ge(added_up, (KT - 1) * (number - 1) + max(1, done - 2))
                elif not first:
                    act.wait_ge(added_up, (KT - 1) * (number - 1))
                act.activation(sq[:, k % 2], src[:, k], ACT.Square).then_inc(squared, 1)

            def x_high(c, k):
                act.activation(xn_hi[:, k], x_next[:, k], ACT.Copy, scale=g_in[:, k:k + 1])\
                    .then_inc(xn_hi_done, 1)

            def copy_r(number):
                act.wait_ge(spread, number)
                act.activation(r_all[:, :], ps_s[:, 1], ACT.Copy).then_inc(r_copied, 1)

            def copy_out(c, j):
                kind, n = ITEMS[j]
                if (kind, n) not in FROM_ACT:
                    return
                act.wait_ge(proj_done, primed(c, N, j + 1))
                if kind in "KVQ":
                    dst = kq_raw[:, KQV.index((kind, n)) % 2]
                    if (kind, n) == ("Q", 1):
                        act.wait_ge(v_turned, at(c, 1, 1))
                else:
                    dst = by_r[:, :]
                    if kind == "G":
                        act.wait_ge(conv_step, primed(c, STEPS_CONV * CONVS, STEPS_CONV * n + 2))
                    else:
                        gates = len([i for i in ITEMS[:j] if i in GATES])
                        act.wait_ge(silu_done, primed(c, len(GATES), gates))
                act.activation(dst, ps_proj[RING3[j]][:, :], ACT.Copy).then_inc(copied, 1)

            def tanh(c, j):
                i = GATES.index(ITEMS[j])
                if i:
                    kind, n = GATES[i - 1]
                    if kind == "G":
                        act.wait_ge(gated, at(c, CONVS, n + 1))
                    else:
                        act.wait_ge(made, primed(c, len(MADE), MADE.index((kind, n)) + 1))
                act.wait_ge(g_scaled, at(c, len(GATES), i + 1))
                act.activation(th[:, :], by_r[:, :], ACT.Tanh, scale=0.5).then_inc(tanh_done, 1)

            def high_part(c, j):
                kind, n = ITEMS[j]
                if kind in "KQ":
                    i = ROPED.index((kind, n))
                    act.wait_ge(rope_step, primed(c, STEPS_ROPE * len(ROPED), STEPS_ROPE * (i + 1)))
                if kind == "K":
                    act.activation(k_st[:, :, 0:P], k_st[:, :, T:T + P].bitcast(F32), ACT.Copy)\
                        .then_inc(kept, 1)
                    act.wait_ge(kept, at(c, 2, 1))
                    for kv in range(N_KV_HEADS):
                        src = rot_a[kv * HEAD_DIM:(kv + 1) * HEAD_DIM, :]
                        for half in range(2):
                            ins = act.activation(k_st[half * HEAD_DIM:(half + 1) * HEAD_DIM, 2 * kv, P:],
                                                 src, ACT.Copy)
                    ins.then_inc(kq_hi, 1)
                elif kind == "Q":
                    act.activation(q_st[0:HEAD_DIM, 2 * n], rot_a[0:HEAD_DIM, :], ACT.Copy)
                    act.activation(q_st[HEAD_DIM:P, 2 * n + 1], rot_a[HEAD_DIM:P, :], ACT.Copy)\
                        .then_inc(kq_hi, 1)
                elif kind in "BA":
                    act.wait_ge(made, primed(c, len(MADE), MADE.index((kind, n)) + 1))
                    act.activation(mix_hi[:, MIX_TILE[kind, n]], made_in((kind, n))[:, :], ACT.Copy, scale=0.5)\
                        .then_inc(mix_hi_done, 1)

            def v_high(c):
                act.wait_ge(v_turned, at(c, 1, 1))
                act.activation(v_st[:, 0], v_st[:, BLOCKS].bitcast(F32), ACT.Copy).then_inc(kept, 1)
                act.wait_ge(kept, at(c, 2, 2))
                act.activation(v_st[:, 1:, :, 0, :],
                               ps_o[:, :].rearrange("p (b k d) -> p b k d", b=BLOCKS, k=N_KV_HEADS),
                               ACT.Copy).then_inc(v_hi, 1)

            def normalize(c, un):
                act.wait_ge(inv_done, at(c, UNITS, un + 1))
                for i in range(GROUP):
                    ins = act.activation(probs[:, i], probs[:, i], ACT.Copy, scale=inv[:, i:i + 1])
                ins.then_inc(p_ready, 1)

            def copy_before(c, un):
                before_keys = ps_s[:, :, :].rearrange("p a (i s k) -> p a i s k", i=2, s=2)[:, :, :, 0]
                dst = probs[:, :, :].rearrange("p (a i) k -> p a i k", a=2)
                if un == 0:
                    act.wait_ge(bias_done, 1)
                act.wait_ge(qk_done, at(c, UNITS, un + 1))
                if un % BLOCKS == 0:
                    act.activation(dst, before_keys, ACT.Identity, bias=before_bias[:, :])\
                        .then_inc(before_copied, 1)
                else:
                    act.activation(dst, before_keys, ACT.Copy).then_inc(before_copied, 1)

            def exps(c, un):
                act.wait_ge(max_done, at(c, UNITS, un + 1))
                for i in range(GROUP):
                    act.activation(probs[:, i], probs[:, i], ACT.Exp, bias=neg_max[:, i:i + 1],
                                   scale=SCALE, accum_out=row_sum[:, i:i + 1])
                act.wait_ge(off_done, at(c, UNITS, un + 1))
                act.activation(sink_exp[:, :], sink_off[:, :], ACT.Exp).then_inc(exp_done, 1)

            def probs_high(c, un):
                act.wait_ge(p_turned, at(c, UNITS, un + 1))
                act.activation(pt_hi[:, 1], ps_t[:, 0].rearrange("p (i q) -> p i q", i=GROUP), ACT.Copy)\
                    .then_inc(pt_hi_done, 1)

            def copy_o(c, un):
                g, b = divmod(un, BLOCKS)
                pair = slice(g * GROUP // 2, (g + 1) * GROUP // 2)
                o = ps_o[:, :].rearrange("p (i e q) -> p i e q", i=GROUP // 2, e=2)
                act.wait_ge(pv_done, at(c, UNITS, un + 1))
                act.activation(attn[HEAD_DIM:P, pair, b * P:(b + 1) * P], o[0:HEAD_DIM, :, 1], ACT.Copy)
                act.activation(attn[0:HEAD_DIM, pair, b * P:(b + 1) * P], o[HEAD_DIM:P, :, 0], ACT.Copy)\
                    .then_inc(o_copied, 1)

            act.sem_inc(copied, len(FROM_ACT))
            act.sem_inc(squared, BY_POOL)
            act.wait_ge(consts_made, 1)
            act.activation(ones[:, :], u_tail[:, 0, 0:1], ACT.Exp).then_inc(one_made, 1)
            act.wait_ge(g_in_sbuf, 16)
            for k in range(KT):
                act.wait_ge(x_first[k], 16)
                x_high(0, k)
                if k == 0:
                    split_w(0, 0)
            split_w(0, 1)
            for k in range(BY_POOL, KT):
                square(1, k, x_next)

            def slots(c, these, edge):
                for s in these:
                    if s + 1 == N and not edge:
                        split_w(c + 1, 0)
                    elif s + 1 < N and s != N_IN and not (s == 0 and edge):
                        split_w(c, s + 1)
                    if s == 3 and edge:
                        high_part(c, 0)
                    if s >= 1:
                        copy_out(c, s - 1)
                    if s >= 2 and s != N_IN + 1 and not (s == 2 and edge):
                        high_part(c, s - 2)
                    if s == N_IN:
                        high_part(c, s - 1)
                        split_w(c, s + 1)
                    if s == V_TURN:
                        v_high(c)
                    if s in TURN_SLOT:
                        probs_high(c, TURN_SLOT.index(s))
                    if s in PV_SLOT:
                        copy_o(c, PV_SLOT.index(s))
                    if s - 1 in QK_SLOT:
                        normalize(c, QK_SLOT.index(s - 1))
                    if s in QK_SLOT:
                        copy_before(c, QK_SLOT.index(s))
                        exps(c, QK_SLOT.index(s))
                    if s >= 1 and ITEMS[s - 1] in GATES:
                        tanh(c, s - 1)
                    if s == 1 and edge:
                        copy_r(1)
                    if s == 0 and not edge:
                        act.wait_ge(h_added, primed(c, KT, 0))
                        square(norm_fin(c - 1), KT - 1, h)
                    if s > N_IN:
                        m = s - N_IN - 1
                        act.wait_ge(h_added, primed(c, KT, m + 1))
                        square(NORMS if edge else norm_fin(c), m, h)
                    if s in SQUARE_SLOT and not edge:
                        k = SQUARE_SLOT.index(s)
                        if k == 0:
                            act.wait_ge(x_in, at(c + 1, 16, 0))
                        square(norm_in(c + 1), k, x_next)
                    if s == COPY_SLOT and not edge:
                        copy_r(norm_in(c + 1))
                    for k in range(KT):
                        if s == HIGH_SLOT[k] and not edge:
                            x_high(c + 1, k)

            by_chunk(act, slots)
            act.wait_ge(added_up, (KT - 1) * (NORMS - 1) + KT - 3)
            for half in range(HALVES):
                act.wait_ge(last_added, half + 1)
                act.activation(sq[:, (KT - 1) % 2, TOKENS[half]], h[:, KT - 1, TOKENS[half]], ACT.Square)\
                    .then_inc(last_squared, 1)

        @block.vector
        def _(dve):
            def split_w(c, j):
                dve.wait_ge(w_hi, at(c, N, j + 1))
                dve.tensor_tensor(w_split[:, j % 2, 1], w_raw[:, RING3[j]],
                                  w_split[:, j % 2, 0].bitcast(F32), ALU.subtract).then_inc(w_lo, 1)

            def add_up(number, k):
                first = isinstance(number, int) and number == 1
                if first and k < BY_POOL:
                    return
                dve.wait_ge(squared, KT * (number - 1) + k + 1)
                if first and k == BY_POOL + 1 or not first and k == 1:
                    dve.tensor_tensor(acc[:, :], sq[:, 0], sq[:, 1], ALU.add).then_inc(added_up, 1)
                elif k > 1 and not (first and k == BY_POOL):
                    done = k - 1 - (BY_POOL if first else 0)
                    dve.wait_ge(added_up, (KT - 1) * (number - 1) + done)
                    dve.tensor_tensor(acc[:, :], acc[:, :], sq[:, k % 2], ALU.add).then_inc(added_up, 1)

            def add_pool_sum():
                dve.wait_ge(pool_squared, 2 * BY_POOL - 1)
                dve.wait_ge(added_up, KT - 1 - BY_POOL)
                dve.tensor_tensor(acc[:, :], acc[:, :], attn[:, 0], ALU.add).then_inc(added_up, BY_POOL)

            def mean_square(number):
                dve.wait_ge(summed, number)
                dve.tensor_scalar(mean[:, :], ps_s[:, 0, 0:BLOCKS], 1.0 / D_MODEL, EPS, ALU.mult, ALU.add)\
                    .then_inc(mean_done, 1)

            def x_low(c, k):
                dve.wait_ge(xn_hi_done, at(c, KT, k + 1))
                dve.scalar_tensor_tensor(xn_lo[:, k], x_next[:, k], g_in[:, k:k + 1],
                                         xn_hi[:, k].bitcast(F32), ALU.mult, ALU.subtract)\
                    .then_inc(xn_lo_done, 1)

            def rotate(c, j):
                kind, n = ITEMS[j]
                i = ROPED.index((kind, n))
                turn = KQV.index((kind, n)) % 2
                done = STEPS_ROPE * i
                per = STEPS_ROPE * len(ROPED)
                src = kq_raw[:, turn]
                if i == 0:
                    dve.wait_ge(rope_scaled, at(c, 1, 1))
                dve.wait_ge(copied, primed(c, len(FROM_ACT), FROM_ACT.index((kind, n)) + 1))
                dve.wait_ge(kq_lo, primed(c, len(ROPED), i))
                half = ROT_DIM // 2
                swap = [p ^ half if p < ROT_DIM else p for p in range(32)]
                dve.tensor_tensor(rot_a[:, :], src, rope_t[:, 0], ALU.mult).then_inc(rope_step, 1)
                dve.stream_shuffle(rot_b[:, :], src, swap).then_inc(rope_step, 1)
                dve.wait_ge(rope_step, primed(c, per, done + 2))
                dve.tensor_tensor(rot_b[:, :], rot_b[:, :], rope_t[:, 1], ALU.mult).then_inc(rope_step, 1)
                dve.wait_ge(rope_step, primed(c, per, done + 3))
                dve.tensor_tensor(rot_a[:, :], rot_a[:, :], rot_b[:, :], ALU.add).then_inc(rope_step, 1)

            def y_free(c, item):
                dve.wait_ge(mix_lo_done, primed(c, len(MADE), MADE.index(item)))

            def convolve(c, n):
                per, done = STEPS_CONV * CONVS, STEPS_CONV * n
                bank = ps_proj[RING3[ITEMS.index(("C", n))]]
                lag = CONV_K - 1
                dve.wait_ge(proj_done, primed(c, N, ITEMS.index(("C", n)) + 1))
                dve.wait_ge(h_scaled, at(c, STEPS_H * CONVS, STEPS_H * (n + 1)))
                dve.wait_ge(conv_step, primed(c, per, done))
                dve.tensor_copy(u[:, 0:lag], u_tail[:, n]).then_inc(conv_step, 1)
                dve.tensor_tensor(u[:, lag:], bank[:, :], by_r[:, :], ALU.mult).then_inc(conv_step, 1)
                dve.wait_ge(conv_step, primed(c, per, done + 2))
                y_free(c, ("A", 2) if n == CONVS - 1 else ("B", n))
                dve.tensor_scalar(y[:, :], u[:, 0:T], taps[:, 0, n:n + 1], None, ALU.mult)\
                    .then_inc(conv_step, 1)
                for j in range(1, CONV_K):
                    dve.wait_ge(conv_step, primed(c, per, done + 2 + j))
                    dve.scalar_tensor_tensor(y[:, :], u[:, j:j + T], taps[:, j, n:n + 1], y[:, :],
                                             ALU.mult, ALU.add).then_inc(conv_step, 1)
                dve.tensor_copy(u_tail[:, n], u[:, T:T + lag]).then_inc(conv_step, 1)

            def gate(c, j):
                kind, n = ITEMS[j]
                i = GATES.index((kind, n))
                dve.wait_ge(tanh_done, at(c, len(GATES), i + 1))
                dve.scalar_tensor_tensor(th[:, :], th[:, :], 1.0, by_r[:, :],
                                         ALU.add, ALU.mult).then_inc(silu_done, 1)
                if kind == "A":
                    dve.wait_ge(o_added, primed(c, UNITS, BLOCKS * (n // (GROUP // 2) + 1)))
                    dve.wait_ge(silu_done, primed(c, len(GATES), i + 1))
                    y_free(c, (kind, n))
                    dve.tensor_tensor(made_in((kind, n))[:, :], th[:, :], attn[:, n], ALU.mult).then_inc(made, 1)
                else:
                    dve.wait_ge(y_scaled, at(c, CONVS, n + 1))
                    dve.wait_ge(silu_done, primed(c, len(GATES), i + 1))
                    dve.tensor_tensor(y[:, :], th[:, :], y[:, :], ALU.mult).then_inc(gated, 1)

            def times_b(c, j):
                n = ITEMS[j][1]
                dve.wait_ge(proj_done, primed(c, N, j + 1))
                dve.wait_ge(gated, at(c, CONVS, n + 1))
                dve.tensor_tensor(y[:, :], ps_proj[RING3[j]][:, :], y[:, :], ALU.mult).then_inc(made, 1)

            def add_h(c, m):
                if m == 0:
                    dve.wait_ge(h_in_sbuf, at(c, 16, 16))
                dve.wait_ge(proj_done, primed(c, N, N_IN + m + 1))
                dve.tensor_tensor(h[:, m], ps_proj[RING3[N_IN + m]][:, :], h[:, m], ALU.add)\
                    .then_inc(h_added, 1)

            def finish(k, done):
                dve.scalar_tensor_tensor(h[:, k], h[:, k], g_fin[:, k:k + 1], ps_t[:, 1], ALU.mult, ALU.mult)\
                    .then_inc(done, 1)

            def low_part(c, j):
                kind, n = ITEMS[j]
                lo, hi = slice(0, HEAD_DIM), slice(HEAD_DIM, P)
                if kind in "KQ":
                    dve.wait_ge(kq_hi, at(c, len(ROPED), ROPED.index((kind, n)) + 1))
                if kind == "K":
                    for kv, from_half in enumerate((lo, hi)):
                        for half in (lo, hi):
                            ins = dve.tensor_tensor(k_st[half, 2 * kv + 1, P:], rot_a[from_half, :],
                                                    k_st[from_half, 2 * kv, P:].bitcast(F32), ALU.subtract)
                    ins.then_inc(kq_lo, 1)
                elif kind == "Q":
                    dve.tensor_tensor(q_st[hi, 2 * n], rot_a[lo, :], q_st[lo, 2 * n].bitcast(F32),
                                      ALU.subtract)
                    dve.tensor_tensor(q_st[lo, 2 * n + 1], rot_a[hi, :], q_st[hi, 2 * n + 1].bitcast(F32),
                                      ALU.subtract).then_inc(kq_lo, 1)
                elif kind in "BA":
                    k = MIX_TILE[kind, n]
                    dve.wait_ge(mix_hi_done, at(c, len(MADE), MADE.index((kind, n)) + 1))
                    dve.scalar_tensor_tensor(mix_lo[:, k], made_in((kind, n))[:, :], 0.5, mix_hi[:, k].bitcast(F32),
                                             ALU.mult, ALU.subtract).then_inc(mix_lo_done, 1)

            def v_low(c):
                dve.wait_ge(v_hi, at(c, 1, 1))
                dve.tensor_tensor(v_st[:, 1:, :, 1, :],
                                  ps_o[:, :].rearrange("p (b k d) -> p b k d", b=BLOCKS, k=N_KV_HEADS),
                                  v_st[:, 1:, :, 0, :].bitcast(F32), ALU.subtract).then_inc(v_lo, 1)

            def maxima(c, un):
                g = un // BLOCKS
                own_keys = ps_s[:, :, :].rearrange("p a (i s k) -> p a i s k", i=2, s=2)[:, :, :, 1]
                wait_alone(dve, before_copied, at(c, UNITS, un + 1), dve_passed)
                dve.copy_predicated(probs[:, :, :].rearrange("p (a i) k -> p a i k", a=2),
                                    own[:, None, None, :].broadcast_to([P, 2, 2, P]), own_keys)\
                    .then_inc(own_copied, 1)
                wait_alone(dve, own_copied, at(c, UNITS, un + 1), dve_passed)
                dve.tensor_reduce(score_max[:, :], probs[:, :, :], mybir.AxisListType.X, ALU.max)\
                    .then_inc(scores_max, 1)
                dve.wait_ge(scores_max, at(c, UNITS, un + 1))
                dve.scalar_tensor_tensor(neg_max[:, :], score_max[:, :], -SCALE,
                                         neg_sink[:, g * GROUP:(g + 1) * GROUP], ALU.mult, ALU.min)\
                    .then_inc(max_done, 1)
                dve.wait_ge(max_done, at(c, UNITS, un + 1))
                dve.tensor_tensor(sink_off[:, :], neg_max[:, :], sink[:, g * GROUP:(g + 1) * GROUP],
                                  ALU.add).then_inc(off_done, 1)

            def denominators(c, un):
                dve.wait_ge(exp_done, at(c, UNITS, un + 1))
                dve.tensor_tensor(denom[:, :], row_sum[:, :], sink_exp[:, :], ALU.add)\
                    .then_inc(denom_done, 1)
                dve.wait_ge(denom_done, at(c, UNITS, un + 1))
                dve.reciprocal(inv[:, :], denom[:, :]).then_inc(inv_done, 1)

            def probs_low(c, un):
                dve.wait_ge(pt_hi_done, at(c, UNITS, un + 1))
                dve.tensor_tensor(pt_lo[:, 1], ps_t[:, 0].rearrange("p (i q) -> p i q", i=GROUP),
                                  pt_hi[:, 1].bitcast(F32), ALU.subtract).then_inc(pt_lo_done, 1)

            def add_o(c, un):
                g, b = divmod(un, BLOCKS)
                pair = slice(g * GROUP // 2, (g + 1) * GROUP // 2)
                o = ps_o[:, :].rearrange("p (i e q) -> p i e q", i=GROUP // 2, e=2)
                dve.wait_ge(o_copied, at(c, UNITS, un + 1))
                for e, half in enumerate((slice(0, HEAD_DIM), slice(HEAD_DIM, P))):
                    dst = attn[half, pair, b * P:(b + 1) * P]
                    ins = dve.tensor_tensor(dst, o[half, :, e], dst, ALU.add)
                ins.then_inc(o_added, 1)

            for primed_sem, per in ((w_lo, N), (rope_step, STEPS_ROPE * len(ROPED)),
                                    (conv_step, STEPS_CONV * CONVS), (finished, KT), (silu_done, len(GATES)),
                                    (made, len(MADE)), (o_added, UNITS), (h_added, KT),
                                    (kq_lo, len(ROPED)), (mix_lo_done, len(MADE))):
                dve.sem_inc(primed_sem, per)
            dve.memset(k_st[:, :, T:T + P].bitcast(F32), 0.0)
            dve.memset(v_st[:, BLOCKS].bitcast(F32), 0.0).then_inc(signs, 1)
            dve.wait_ge(g_in_sbuf, 16)
            x_low(0, 0)
            split_w(0, 0)
            for k in range(1, KT):
                x_low(0, k)
            split_w(0, 1)
            for k in range(BY_POOL + 1, KT):
                add_up(1, k)
            add_pool_sum()

            def slots(c, these, edge):
                for s in these:
                    if s - 1 in QK_SLOT:
                        denominators(c, QK_SLOT.index(s - 1))
                    if s + 1 == N and not edge:
                        split_w(c + 1, 0)
                    elif s + 1 < N and s != N_IN and not (s == 0 and edge):
                        split_w(c, s + 1)
                    if s == 1 and edge:
                        mean_square(1)
                        dve.wait_ge(consts_in, 32)
                        dve.tensor_scalar(neg_sink[:, :], sink[:, :], -1.0, None, ALU.mult).then_inc(signs, 1)
                        dve.wait_ge(signs, 2)
                    if s < 2 and not edge:
                        add_up(norm_fin(c - 1), KT - 2 + s)
                    if s == 0 and not edge:
                        add_h(c - 1, KT - 1)
                    if s > N_IN + 2:
                        add_up(NORMS if edge else norm_fin(c), s - N_IN - 2)
                    if s > N_IN:
                        add_h(c, s - N_IN - 1)
                    if s - 1 in SQUARE_SLOT[1:] and not edge:
                        add_up(norm_in(c + 1), SQUARE_SLOT.index(s - 1))
                    if s in TURN_SLOT:
                        probs_low(c, TURN_SLOT.index(s))
                    if s in QK_SLOT:
                        maxima(c, QK_SLOT.index(s))
                    if s in PV_SLOT:
                        add_o(c, PV_SLOT.index(s))
                    if s == 2 and edge:
                        rotate(c, 0)
                    if s == 3 and edge:
                        low_part(c, 0)
                    if s >= 2 and s != N_IN + 1 and not (s == 2 and edge):
                        low_part(c, s - 2)
                    if s >= 1:
                        kind, n = ITEMS[s - 1]
                        if kind in "KQ" and not (s == 1 and edge):
                            rotate(c, s - 1)
                        elif kind == "C":
                            convolve(c, n)
                        elif kind in "GA":
                            gate(c, s - 1)
                        elif kind == "B":
                            times_b(c, s - 1)
                    if s == N_IN:
                        low_part(c, s - 1)
                        split_w(c, s + 1)
                    if s == V_TURN:
                        v_low(c)
                    if s == R_SUM_SLOT and not edge:
                        mean_square(norm_fin(c - 1))
                    if s == SUM_SLOT and not edge:
                        mean_square(norm_in(c + 1))
                    for k in range(KT):
                        if s == FINISH_SLOT[k] and not edge:
                            if k == 0:
                                dve.wait_ge(spread, norm_fin(c - 1))
                            finish(k, finished)
                        if s == LOW_SLOT[k] and not edge:
                            x_low(c + 1, k)

            by_chunk(dve, slots)
            add_up(NORMS, KT - 2)

            def add_last(half):
                dve.wait_ge(last_product, half + 1)
                dve.tensor_tensor(h[:, KT - 1, TOKENS[half]], LAST_BANK[half][:, TOKENS[half]],
                                  h[:, KT - 1, TOKENS[half]], ALU.add).then_inc(last_added, 1)

            def mean_last(half):
                dve.wait_ge(last_summed, half + 1)
                dve.tensor_scalar(mean[:, TILES[half]], ps_s[:, 0, TILES[half]], 1.0 / D_MODEL, EPS, ALU.mult,
                                  ALU.add).then_inc(last_mean, 1)

            def finish_last(half, tiles):
                dve.wait_ge(last_spread, half + 1)
                for k in tiles:
                    dve.scalar_tensor_tensor(h[:, k, TOKENS[half]], h[:, k, TOKENS[half]], g_fin[:, k:k + 1],
                                             LAST_R[half][:, TOKENS[half]], ALU.mult, ALU.mult)\
                        .then_inc(last_finished, 1)

            add_last(0)
            mean_last(0)
            add_last(1)
            finish_last(0, range(BETWEEN))
            mean_last(1)
            finish_last(0, range(BETWEEN, KT))
            finish_last(1, range(KT))

        @block.tensor
        def _(pe):
            def product(c, j, inside, half=None):
                kind, n = ITEMS[j]
                i, back = before(j)
                pe.wait_ge(w_lo, primed(c, N, j + 1))
                bank_free, per, k = released(i)
                pe.wait_ge(bank_free, primed(c, per, k - per * back))
                dst, tokens, done = ps_proj[RING3[j]][:, :], slice(0, T), proj_done
                if half is not None:
                    dst, tokens, done = LAST_BANK[half][:, TOKENS[half]], TOKENS[half], last_product
                    pe.wait_ge(o_added, primed(c, UNITS, UNITS))
                hi, lo = (mix_hi, mix_lo) if kind == "O" else (xn_hi, xn_lo)
                order = [MIX_TILE[i] for i in MADE] if kind == "O" else range(KT)
                for a, k in enumerate(order):
                    if j == 0:
                        pe.wait_ge(xn_lo_done, at(c, KT, k + 1))
                    for step in inside.get(a, ()):
                        step()
                    if kind == "O" and n == 0:
                        pe.wait_ge(mix_lo_done, primed(c, len(MADE), a + 1))
                    for b, (w, v) in enumerate(((0, hi), (0, lo), (1, hi))):
                        mm = pe.matmul(dst, w_split[:, j % 2, w, k], v[:, k, tokens],
                                       start=a == 0 and b == 0, stop=a == KT - 1 and b == 2)
                mm.then_inc(done, 1)

            def turn_v(c):
                pe.wait_ge(v_scaled, at(c, 1, 1))
                pe.wait_ge(o_added, primed(c, UNITS, 0))
                for b in range(BLOCKS):
                    mm = pe.transpose(ps_o[:, b * P:(b + 1) * P], kq_raw[:, 1, b * P:(b + 1) * P], ident[:, :])
                mm.then_inc(v_turned, 1)

            def scores(c, un):
                g, b = divmod(un, BLOCKS)
                pe.wait_ge(kq_lo, primed(c, len(ROPED), 1 + (g + 1) * GROUP // 2))
                if un == 0:
                    pe.wait_ge(mean_done, at(c, 2, 1))
                    pe.wait_ge(r_copied, at(c, 1, 1))
                else:
                    pe.wait_ge(own_copied, at(c, UNITS, un))
                for i in range(GROUP):
                    for part in range(2):
                        mm = pe.matmul(ps_s[:, i // 2, (i % 2) * 2 * P:(i % 2 + 1) * 2 * P],
                                       q_st[:, g * GROUP + i, b * P:(b + 1) * P],
                                       k_st[:, 2 * g + part, b * P:(b + 2) * P],
                                       start=part == 0, stop=part == 1)
                mm.then_inc(qk_done, 1)

            def turn_p(c, un):
                pe.wait_ge(p_ready, at(c, UNITS, un + 1))
                for i in range(GROUP):
                    mm = pe.transpose(ps_t[:, 0, i * P:(i + 1) * P], probs[:, i], ident[:, :])
                mm.then_inc(p_turned, 1)

            def values(c, un):
                g, b = divmod(un, BLOCKS)
                if un == 0:
                    pe.wait_ge(v_lo, at(c, 1, 1))
                else:
                    pe.wait_ge(o_added, primed(c, UNITS, un))
                for kb in range(2):
                    pe.wait_ge(triangle, at(c, STEPS_TRIANGLE * UNITS, STEPS_TRIANGLE * un + 2 * (kb + 1)))
                    for part, pt in enumerate((pt_hi, pt_lo)):
                        mm = pe.matmul(ps_o[:, :],
                                       v_st[:, b + kb, g].rearrange("p a d -> p (a d)"),
                                       pt[:, kb].rearrange("p i q -> p (i q)"),
                                       start=kb == 0 and part == 0, stop=kb == 1 and part == 1)
                mm.then_inc(pv_done, 1)

            def sums(number):
                pe.wait_ge(added_up, (KT - 1) * number)
                for t in range(BLOCKS):
                    mm = pe.matmul(ps_s[:, 0, t:t + 1], acc[:, t * P:(t + 1) * P], ones[:, :],
                                   start=True, stop=True)
                mm.then_inc(summed, 1)

            def sums_last(half):
                pe.wait_ge(added_up, (KT - 1) * (NORMS - 1) + KT - 2)
                pe.wait_ge(last_squared, half + 1)
                if half:
                    pe.wait_ge(last_mean, half)
                for t in range(BLOCKS)[TILES[half]]:
                    for i, part in enumerate((acc[:, :], sq[:, (KT - 1) % 2])):
                        mm = pe.matmul(ps_s[:, 0, t:t + 1], part[:, t * P:(t + 1) * P], ones[:, :],
                                       start=i == 0, stop=i == 1)
                mm.then_inc(last_summed, 1)

            def spread_last(half):
                pe.wait_ge(last_r, half + 1)
                for t in range(BLOCKS)[TILES[half]]:
                    mm = pe.transpose(LAST_R[half][:, t * P:(t + 1) * P], r[:, t:t + 1].broadcast_to([P, P]),
                                      ident[:, :])
                mm.then_inc(last_spread, 1)

            def spread_r(number, dst):
                pe.wait_ge(r_done, number)
                for t in range(BLOCKS):
                    mm = pe.transpose(dst[:, t * P:(t + 1) * P], r[:, t:t + 1].broadcast_to([P, P]), ident[:, :])
                mm.then_inc(spread, 1)

            pe.sem_inc(proj_done, N)
            pe.wait_ge(signs, 1)
            for _ in range(WARM_UP):
                pe.matmul(ps_t[:, 0], k_st[:, 0, T:T + P], k_st[:, :, T:T + P], start=True, stop=True)
            pe.wait_ge(one_made, 1)
            pe.wait_ge(consts_made, 6)

            def slots(c, these, edge):
                for s in these:
                    if s == R_SUM_SLOT and not edge:
                        sums(norm_fin(c - 1))
                    if s == V_TURN:
                        turn_v(c)
                    inside = {}
                    if s in TURN_SLOT:
                        inside[TURN_AT] = [lambda: turn_p(c, TURN_SLOT.index(s))]
                    if s in PV_SLOT:
                        inside[PV_AT] = [lambda: values(c, PV_SLOT.index(s))]
                    if s == 1 and edge:
                        inside[SUM_AT] = [lambda: sums(1)]
                    if s == 2 and edge:
                        inside[0] = [lambda: spread_r(1, ps_s[:, 1])]
                    if s in QK_SLOT:
                        scores(c, QK_SLOT.index(s))
                    if s == SUM_SLOT and not edge:
                        sums(norm_in(c + 1))
                    if s == R_SPREAD_SLOT and not edge:
                        spread_r(norm_fin(c - 1), ps_t[:, 1])
                    if s == SPREAD_SLOT and not edge:
                        spread_r(norm_in(c + 1), ps_s[:, 1])
                    if s < N - 1 or not edge:
                        product(c, s, inside)

            by_chunk(pe, slots)
            product(CHUNKS - 1, N - 1, {}, 0)
            product(CHUNKS - 1, N - 1, {LAST_SUM_AT: [lambda: sums_last(0)]}, 1)
            spread_last(0)
            sums_last(1)
            spread_last(1)


def rope_tables():
    import numpy as np
    half = ROT_DIM // 2
    inv_freq = np.float32(500000.0) ** (-np.arange(0, ROT_DIM, 2, dtype=np.float32) / np.float32(ROT_DIM))
    ang = np.arange(SEQ, dtype=np.float32)[None, :] * inv_freq.astype(np.float32)[:, None]
    cos, sin = np.cos(ang.astype(np.float64)), np.sin(ang.astype(np.float64))
    table = np.zeros((2, HEAD_DIM, SEQ), np.float64)
    table[0] = 1.0
    table[0, :ROT_DIM] = np.concatenate([cos, cos])
    table[1, :ROT_DIM] = np.concatenate([-sin, sin])
    table = np.concatenate([table] * (P // HEAD_DIM), axis=1).reshape(2, P, CHUNKS, T)
    return np.ascontiguousarray(table.transpose(1, 2, 0, 3).astype(np.float32))


def kernel(**inputs):
    import numpy as np
    import concourse.bacc as bacc
    from concourse.bass_utils import run_bass_kernel_spmd

    v = {name: np.asarray(a) for name, a in inputs.items()}

    def items(w):
        return w.reshape(KT, P, -1, P).transpose(2, 1, 0, 3)

    tiles = {"O": items(v["w_out"]), **{kind: items(v["w_in"])[col:] for kind, col in COL.items()}}
    laid_out = {
        "x_t": v["x"].reshape(CHUNKS, T, KT, P).transpose(0, 3, 2, 1),
        "g_in_t": v["norm_g"].reshape(KT, P).T,
        "w_items": np.stack([tiles[kind][n] for kind, n in ITEMS]),
        "sinks": v["sinks"],
        "taps_t": v["conv_w"].reshape(CONV_K, CONVS, P).transpose(2, 0, 1),
        "g_fin_t": v["final_g"].reshape(KT, P).T,
        "rope": rope_tables(),
    }
    nc = bacc.Bacc("TRN2", target_bir_lowering=False, num_devices=1)
    arrays, args = {}, []
    for name, a in laid_out.items():
        a = np.ascontiguousarray(a)
        arrays[f"in_{name}"] = a
        args.append(nc.dram_tensor(f"in_{name}", a.shape, mybir.dt.from_np(a.dtype), kind="ExternalInput").ap())
    args.append(nc.dram_tensor("out_0", (CHUNKS, P, KT, T), F32, kind="ExternalOutput").ap())
    hybrid_layer(nc, *args)
    r = run_bass_kernel_spmd(nc, [arrays], core_ids=[0])
    return r.results[0]["out_0"].transpose(0, 3, 2, 1).reshape(1, SEQ, D_MODEL)
```
